# Optimizing a Trainium2 kernel written in Bass

```python
import math
import jax, jax.numpy as jnp
from jax import lax
import numpy as np

D_MODEL = 2048
BATCH = 1
SEQ = 512
DEPTH = 1

HEAD_DIM = 64
N_Q_HEADS = 16
N_KV_HEADS = 2
GROUP = N_Q_HEADS // N_KV_HEADS
WINDOW = 128
BLOCK = 128
ROT_DIM = HEAD_DIM // 4
ROPE_THETA = 500000.0
Q_W = N_Q_HEADS * HEAD_DIM
KV_W = N_KV_HEADS * HEAD_DIM

SSM_W = D_MODEL // 2
SSM_GC = 16
SSM_G = SSM_W // SSM_GC
SSM_P = 64

D_FF = 4 * D_MODEL

MIX_W = Q_W + SSM_W
IN_W = Q_W + 2 * KV_W + SSM_W + 2 * D_MODEL
EPS = 1e-6

kernel_name = "hybrid_swa_sink_s5_gated_block"

def rms_norm(x, g):
    xf = x.astype(jnp.float32)
    y = xf * lax.rsqrt(jnp.mean(xf * xf, axis=-1, keepdims=True) + EPS)
    return (y * g.astype(jnp.float32)).astype(x.dtype)

def partial_rope(x, pos):
    half = ROT_DIM // 2
    inv = ROPE_THETA ** (-jnp.arange(half, dtype=jnp.float32) * 2.0 / ROT_DIM)
    ang = pos.astype(jnp.float32)[:, None] * inv[None, :]
    cos = jnp.cos(ang)[None, :, None, :]
    sin = jnp.sin(ang)[None, :, None, :]
    xr = x[..., :ROT_DIM].astype(jnp.float32)
    x1, x2 = xr[..., :half], xr[..., half:]
    rot = jnp.concatenate([x1 * cos - x2 * sin, x2 * cos + x1 * sin], axis=-1)
    return jnp.concatenate([rot.astype(x.dtype), x[..., ROT_DIM:]], axis=-1)

def sliding_window_gqa_sinks(q, k, v, sinks):
    B, L = q.shape[0], q.shape[1]
    nb = L // BLOCK
    qb = q.reshape(B, nb, BLOCK, N_KV_HEADS, GROUP, HEAD_DIM)
    pad = jnp.zeros((B, BLOCK, N_KV_HEADS, HEAD_DIM), k.dtype)
    kp = jnp.concatenate([pad, k], axis=1)
    vp = jnp.concatenate([pad, v], axis=1)
    shp = (B, nb, BLOCK, N_KV_HEADS, HEAD_DIM)
    kb = jnp.concatenate([kp[:, :-BLOCK].reshape(shp), kp[:, BLOCK:].reshape(shp)], axis=2)
    vb = jnp.concatenate([vp[:, :-BLOCK].reshape(shp), vp[:, BLOCK:].reshape(shp)], axis=2)
    s = jnp.einsum('bnqhgd,bnkhd->bnhgqk', qb, kb).astype(jnp.float32) / math.sqrt(HEAD_DIM)
    qi = jnp.arange(BLOCK)[:, None]
    kj = jnp.arange(2 * BLOCK)[None, :]
    rel = qi + BLOCK - kj
    kpos = jnp.arange(nb)[:, None, None] * BLOCK - BLOCK + kj[None]
    mask = (rel >= 0)[None] & (rel < WINDOW)[None] & (kpos >= 0)
    s = jnp.where(mask[None, :, None, None], s, jnp.finfo(jnp.float32).min)
    sink = jnp.broadcast_to(
        sinks.astype(jnp.float32).reshape(N_KV_HEADS, GROUP)[None, None, :, :, None, None],
        s.shape[:-1] + (1,))
    p = jax.nn.softmax(jnp.concatenate([s, sink], axis=-1), axis=-1)[..., :-1]
    o = jnp.einsum('bnhgqk,bnkhd->bnqhgd', p.astype(v.dtype), vb)
    return o.reshape(B, L, Q_W)

def s5_mixer(u, lam_re, lam_im, log_dt, b_re, b_im, c_re, c_im, d_skip, w_glu):
    B, L = u.shape[0], u.shape[1]
    f32 = jnp.float32
    ug = u.reshape(B, L, SSM_G, SSM_GC).astype(f32)
    lr, li = lam_re.astype(f32), lam_im.astype(f32)
    dt = jnp.exp(log_dt.astype(f32))[:, None]
    mag = jnp.exp(lr * dt)
    a_re, a_im = mag * jnp.cos(li * dt), mag * jnp.sin(li * dt)
    den = lr * lr + li * li
    nr, ni = a_re - 1.0, a_im
    coef_re = (nr * lr + ni * li) / den
    coef_im = (ni * lr - nr * li) / den
    br, bi = b_re.astype(f32), b_im.astype(f32)
    bb_re = coef_re[..., None] * br - coef_im[..., None] * bi
    bb_im = coef_re[..., None] * bi + coef_im[..., None] * br
    bu_re = jnp.einsum('blgc,gpc->blgp', ug, bb_re)
    bu_im = jnp.einsum('blgc,gpc->blgp', ug, bb_im)
    at_re = jnp.broadcast_to(a_re, bu_re.shape)
    at_im = jnp.broadcast_to(a_im, bu_im.shape)

    def combine(e1, e2):
        ar1, ai1, br1, bi1 = e1
        ar2, ai2, br2, bi2 = e2
        return (ar2 * ar1 - ai2 * ai1,
                ar2 * ai1 + ai2 * ar1,
                ar2 * br1 - ai2 * bi1 + br2,
                ar2 * bi1 + ai2 * br1 + bi2)

    _, _, xs_re, xs_im = lax.associative_scan(combine, (at_re, at_im, bu_re, bu_im), axis=1)
    y = (jnp.einsum('blgp,gcp->blgc', xs_re, c_re.astype(f32))
         - jnp.einsum('blgp,gcp->blgc', xs_im, c_im.astype(f32))
         + d_skip.astype(f32)[None, None] * ug)
    y = jax.nn.gelu(y.reshape(B, L, SSM_W)).astype(u.dtype)
    zg = y @ w_glu
    return zg[..., :SSM_W] * jax.nn.sigmoid(zg[..., SSM_W:])

def setup_inputs(seed: int = 0) -> dict:
    key = jax.random.key(seed)
    ks = jax.random.split(key, 24)
    f32 = jnp.float32
    nrm = lambda k, shp, s: jax.random.normal(k, shp, f32) * s
    x = jax.random.normal(ks[0], (BATCH, SEQ, D_MODEL), f32)
    gain = lambda k: 1.0 + nrm(k, (DEPTH, D_MODEL), 0.02)
    n_idx = jnp.arange(SSM_P, dtype=f32)
    lam_re = -0.5 + nrm(ks[9], (DEPTH, SSM_G, SSM_P), 0.01)
    lam_im = jnp.pi * n_idx[None, None, :] + nrm(ks[10], (DEPTH, SSM_G, SSM_P), 0.01)
    log_dt = jax.random.uniform(ks[11], (DEPTH, SSM_G), f32, math.log(1e-3), math.log(1e-1))
    return {
        "x": x,
        "norm_mix_pre": gain(ks[1]),
        "norm_mix_post": gain(ks[2]),
        "norm_mlp_pre": gain(ks[3]),
        "norm_mlp_post": gain(ks[4]),
        "w_in": nrm(ks[5], (DEPTH, D_MODEL, IN_W), D_MODEL ** -0.5),
        "sinks": nrm(ks[6], (DEPTH, N_Q_HEADS), 0.5),
        "lam_re": lam_re,
        "lam_im": lam_im,
        "log_dt": log_dt,
        "b_re": nrm(ks[12], (DEPTH, SSM_G, SSM_P, SSM_GC), (2 * SSM_GC) ** -0.5),
        "b_im": nrm(ks[13], (DEPTH, SSM_G, SSM_P, SSM_GC), (2 * SSM_GC) ** -0.5),
        "c_re": nrm(ks[14], (DEPTH, SSM_G, SSM_GC, SSM_P), (2 * SSM_P) ** -0.5),
        "c_im": nrm(ks[15], (DEPTH, SSM_G, SSM_GC, SSM_P), (2 * SSM_P) ** -0.5),
        "d_skip": nrm(ks[16], (DEPTH, SSM_G, SSM_GC), 1.0),
        "w_glu": nrm(ks[17], (DEPTH, SSM_W, 2 * SSM_W), SSM_W ** -0.5),
        "w_branch": nrm(ks[18], (DEPTH, MIX_W, D_MODEL), (MIX_W // 2) ** -0.5),
        "w_out": nrm(ks[19], (DEPTH, D_MODEL, D_MODEL), D_MODEL ** -0.5),
        "w_up": nrm(ks[20], (DEPTH, D_MODEL, D_FF), D_MODEL ** -0.5),
        "w_down": nrm(ks[21], (DEPTH, D_FF, D_MODEL), D_FF ** -0.5),
    }

def reference(x, norm_mix_pre, norm_mix_post, norm_mlp_pre, norm_mlp_post, w_in, sinks,
              lam_re, lam_im, log_dt, b_re, b_im, c_re, c_im, d_skip, w_glu,
              w_branch, w_out, w_up, w_down):
    B, L, _ = x.shape
    pos = jnp.arange(L)
    o1 = Q_W
    o2 = o1 + KV_W
    o3 = o2 + KV_W
    o4 = o3 + SSM_W
    o5 = o4 + D_MODEL
    for l in range(DEPTH):
        h = rms_norm(x, norm_mix_pre[l])
        z = h @ w_in[l]
        q = z[..., :o1].reshape(B, L, N_Q_HEADS, HEAD_DIM)
        k = z[..., o1:o2].reshape(B, L, N_KV_HEADS, HEAD_DIM)
        v = z[..., o2:o3].reshape(B, L, N_KV_HEADS, HEAD_DIM)
        u = z[..., o3:o4]
        g_attn = jax.nn.sigmoid(z[..., o4:o5].astype(jnp.float32)).astype(x.dtype)
        g_ssm = jax.nn.sigmoid(z[..., o5:].astype(jnp.float32)).astype(x.dtype)
        q = partial_rope(q, pos)
        k = partial_rope(k, pos)
        o_attn = sliding_window_gqa_sinks(q, k, v, sinks[l])
        o_ssm = s5_mixer(u, lam_re[l], lam_im[l], log_dt[l], b_re[l], b_im[l],
                         c_re[l], c_im[l], d_skip[l], w_glu[l])
        y_attn = o_attn @ w_branch[l][:Q_W]
        y_ssm = o_ssm @ w_branch[l][Q_W:]
        mixed = (g_attn * y_attn + g_ssm * y_ssm) @ w_out[l]
        x = x + rms_norm(mixed, norm_mix_post[l])
        h2 = rms_norm(x, norm_mlp_pre[l])
        a = jax.nn.relu(h2 @ w_up[l])
        x = x + rms_norm((a * a) @ w_down[l], norm_mlp_post[l])
    return x


_drawn_inputs = setup_inputs


def setup_inputs(seed=0):
    import zlib

    import numpy as np

    out = dict(_drawn_inputs(seed))
    spreads = {}
    factors = {'norm_mix_pre': 2.876,
     'norm_mix_post': 3.72,
     'norm_mlp_pre': 14.307,
     'norm_mlp_post': 52.522,
     'sinks': 6.081,
     'lam_re': 200.0,
     'lam_im': 38.0,
     'log_dt': 39.944,
     'b_re': 52.896,
     'b_im': 52.96,
     'c_re': 52.76,
     'c_im': 53.168}
    for name, (base, spread) in spreads.items():
        noise = np.random.default_rng([zlib.crc32(name.encode()), seed]).standard_normal(out[name].shape)
        drawn = base * np.exp(spread * noise) if base else spread * noise
        out[name] = __import__('jax').numpy.asarray(drawn.astype(out[name].dtype))
    for name, factor in factors.items():
        out[name] = (out[name] * factor).astype(out[name].dtype)
    return out
```

```python
from contextlib import ExitStack

import numpy as np

import concourse.bass as bass
from concourse import mybir

F32 = mybir.dt.float32
F32R = mybir.dt.float32r
I32 = mybir.dt.int32
ALU = mybir.AluOpType
ACT = mybir.ActivationFunctionType
AX = mybir.AxisListType.X

P = 128
T = 512
D = 2048
FF = 4 * D
HEAD = 64
N_Q, N_KV = 16, 2
SSM_W, SSM_G, SSM_C, SSM_S = 1024, 64, 16, 64
ROT, THETA = 16, 500000.0
EPS = 1e-6
KT = D // P
CT = SSM_W // P
ST = SSM_G * SSM_S // P
NW = SSM_S * CT
NP = NW + ST
RING = 4
EJ = 32
NPOW = 9

U_Q, U_U, U_GATE = 0, 20, 36
U_GLU, U_BR, U_OUT, U_UP = 100, 116, 148, 180
U_MLP = U_UP + 8
N_GROUP = FF // 512
U_TAIL = U_MLP + 16 * (N_GROUP - 1)
N_UNIT = U_TAIL + 8
B_GATE, B_GLU, B_BR, B_OUT, B_UP = 9, 25, 33, 49, 57
B_MLP = B_UP + 2
B_TAIL = B_MLP + 10 * (N_GROUP - 1)
N_SLOT0 = 24

LOG2E = 1.4426950408889634
LN2_HI, LN2_LO = 0.693359375, -2.12194440e-4
MAGIC = 12582912.0
EXP_COEF = [1 / 5040., 1 / 720., 1 / 120., 1 / 24., 1 / 6., 0.5, 1.0]
TWO_PI = (6.28125, 0.00193500518798828125, 3.0199159819e-7)
PI_SAFE = 3.1415925


class Count:

    def __init__(self, sem):
        self.sem, self.n, self.turn, self.per = sem, 0, None, 0

    def value(self):
        return self.n if self.turn is None else self.turn * self.per + self.n

    def enter(self, turn, first, per):
        self.turn, self.per, self.at = turn, per, self.n
        self.n -= first * per

    def leave(self, first, end):
        done = self.n + first * self.per - self.at
        assert done == self.per, f"{self.sem}: {done} a turn, {self.per} given"
        self.n = self.at + (end - first) * self.per
        self.turn, self.per = None, 0


def build(nc, wstream, xT, gains, params, b_pad, c_pad, consts, cols, out):
    gate_dram = nc.dram_tensor("gate_scratch", [16, P, 2 * T], F32, kind="Internal").ap()
    x1_dram = nc.dram_tensor("x1_scratch", [8, P, 2 * T], F32, kind="Internal").ap()
    base = (nc.sbuf_base + 31) // 32 * 32

    def at(name, shape, kib, dt=F32):
        return nc.alloc_sbuf_tensor_at(name, [P] + shape, dt, offset=base + int(kib * 1024))

    RAW = at("w_raw", [RING, 4, 256], 0)
    WH = at("w_hi", [RING, 4, 256], 16, F32R)
    WL = at("w_lo", [RING, 4, 256], 32, F32R)
    HH = at("h_hi", [KT, T], 48, F32R)
    HL = at("h_lo", [KT, T], 80, F32R)
    YH = at("y_hi", [CT, T], 48, F32R)
    YL = at("y_lo", [CT, T], 64, F32R)
    OSH = at("o_ssm_hi", [CT, T], 80, F32R)
    OSL = at("o_ssm_lo", [CT, T], 96, F32R)
    ML = at("m_lo", [KT, T], 48, F32R)
    Z = at("mixed", [KT, T], 80)
    ACC = at("mlp_acc", [KT, T], 80)
    XT = at("x_ring", [2, 4, T], 112)
    U = at("u", [CT, T], 112)
    Q = at("q", [8, T], 128)
    MH = at("m_hi", [KT, T], 112, F32R)
    X1F = at("x1_all", [KT, T], 112)
    NPB = 12
    PB = at("probs", [NPB, 2, 256], 144)
    PTB = at("probs_t", [4, T], 168)
    ROPE = at("rope", [2, T], 168)
    KV = at("kv_raw", [2, T], 172)
    SQX = at("x_squares", [2, T], 172)
    KTOK = at("k_t", [P + T], 176)
    VTOK = at("v_tok", [5, P], 178.5)
    MASK = at("mask", [2, 256], 181)
    SUM0 = at("square_sum", [T], 183)
    STD0 = at("std_first", [T], 185)
    E32 = at("rotation_start", [ST, 2, EJ], 183)
    BB = at("b_bar", [CT, 2, P], 191)
    tmp = [at(f"param{k}", [NP], 144 + 2.125 * k) for k in range(11)]
    BT = [at(f"b_bar_tmp{k}", [CT, P], 152 + 4 * k) for k in range(2)]
    ROT_T = at("rotation", [2, T], 144)
    M1 = at("prod_cos", [2, T], 148)
    M2 = at("prod_sin", [2, T], 152)
    WI = at("scan_in", [2, T], 156)
    WO = at("scan_out", [2, T], 160)
    SB = at("states", [2, 2, T], 164)
    GS = at("gate_stage", [2, 2, T], 172)
    US = at("u_stage", [T], 180)
    OAH = at("o_attn_hi", [CT, T], 144, F32R)
    OAL = at("o_attn_lo", [CT, T], 160, F32R)
    SG = at("glu_gate", [T], 176)
    OT = at("glu_out", [T], 178)
    GA = at("gate_attn", [2, T], 180)
    GB = at("gate_ssm", [2, T], 184)
    TA = at("branch_attn", [2, T], 188)
    TB = at("branch_sum", [2, T], 192)
    SQ = at("squares", [2, 2, T], 176)
    SQS = at("square_sums", [2, T], 184)
    XR = at("x_again", [2, 2, T], 160)
    X1 = at("x1", [2, 2, T], 168)
    AH = at("a_hi", [2, 4, T], 144, F32R)
    AL = at("a_lo", [2, 4, T], 160, F32R)
    TT = at("up_normed", [2, T], 188)
    AA = at("a", [2, T], 192)
    RSTD = at("rstd", [T], 199)
    IDENT = at("ident", [P], 201)
    PERM = at("perm", [P], 201.5)
    ONES = at("ones", [P], 202)
    BST = at("b_stage", [2, P], 202.5)
    CST = at("c_stage", [4, 2, 32], 203.5)
    PW = at("powers", [NPOW, 2, ST], 204.5)
    MAG = at("decay", [ST], 206.75)
    GAIN = at("gain", [4, KT], 206.875)
    COLS = at("cols", [32], 207.125)
    SM = at("softmax_cols", [8, 4], 207.25)
    MX = at("softmax_max", [8, 2], 207.375)
    SMK = at("softmax_sink", [8, 2], 207.4375)
    RS = at("softmax_sum", [8, 2], 207.5)
    assert 207.5625 * 1024 + base <= nc.sbuf_usable_end
    D_SKIP, SINK, EPS_C = 0, 8, 24

    with ExitStack() as ctx:
        main = ctx.enter_context(nc.psum_tensor("main", [P, 4, T], F32))
        side = ctx.enter_context(nc.psum_tensor("side", [P, 4, T], F32))

        def sem(name):
            return ctx.enter_context(nc.semaphore(name))

        raw_landed = [sem(f"raw_landed{s}") for s in range(RING)]
        hi_ready, lo_ready, unit_done = sem("hi_ready"), sem("lo_ready"), sem("unit_done")
        bank_read = sem("bank_read")
        x_landed = [sem(f"x_landed{s}") for s in range(2)]
        consts_landed, small_landed, par_landed, b_landed = (
            sem("consts_landed"), sem("small_landed"), sem("par_landed"), sem("b_landed"))
        ones_set, pads_set = sem("ones_set"), sem("pads_set")
        xh_ready, xsq_ready, xl_ready, xsum_step = (
            sem("xh_ready"), sem("xsq_ready"), sem("xl_ready"), sem("xsum_step"))
        stat_done, std_ready = sem("stat_done"), sem("std_ready")
        rope_mm, rope_free, vt_done, v_ready = (
            sem("rope_mm"), sem("rope_free"), sem("vt_done"), sem("v_ready"))
        angle_ready, trig_ready, bb_ready = sem("angle_ready"), sem("trig_ready"), sem("bb_ready")
        scores_done, scores_read, exp_ready, nmax_ready, probs_ready = (
            sem("scores_done"), sem("scores_read"), sem("exp_ready"), sem("nmax_ready"), sem("probs_ready"))
        trans_done, pt_ready, pv_done, o_ready = (
            sem("trans_done"), sem("pt_ready"), sem("pv_done"), sem("o_ready"))
        stage_ready, bu_done, bu_read, state_ready, c_done, y_read, y_ready = (
            sem("stage_ready"), sem("bu_done"), sem("bu_read"), sem("state_ready"),
            sem("c_done"), sem("y_read"), sem("y_ready"))
        c_landed, gate_ready, gate_stored = (
            sem("c_landed"), sem("gate_ready"), [sem("gate_stored0"), sem("gate_stored1")])
        yh_ready, yl_ready, oah_ready, oal_ready = (
            sem("yh_ready"), sem("yl_ready"), sem("oah_ready"), sem("oal_ready"))
        sig_ready, osh_ready, osl_ready = sem("sig_ready"), sem("osh_ready"), sem("osl_ready")
        ga_landed, gb_landed, br_ready, mh_ready, ml_ready = (
            sem("ga_landed"), sem("gb_landed"), sem("br_ready"), sem("mh_ready"), sem("ml_ready"))
        sq_ready, sq_used, sum_ready = sem("sq_ready"), sem("sq_used"), sem("sum_ready")
        xr_landed = [sem("xr_landed0"), sem("xr_landed1")]
        x1_ready, x1_stored, h2h_ready, h2l_ready = (
            sem("x1_ready"), [sem("x1_stored0"), sem("x1_stored1")], sem("h2h_ready"), sem("h2l_ready"))
        h2sq_ready, h2sq_used = sem("h2sq_ready"), sem("h2sq_used")
        a_ready, ah_ready, al_ready = sem("a_ready"), sem("ah_ready"), sem("al_ready")
        fsq_ready, fsq_used, x1_back, out_ready, out_stored = (
            sem("fsq_ready"), sem("fsq_used"), sem("x1_back"), sem("out_ready"), sem("out_stored"))
        dve_step = sem("dve_step")

        block = ctx.enter_context(nc.Block())

        def units_of(slot, first):
            g = slot - first
            return range(4 * g, 4 * g + 4) if 0 <= g < 8 else ()

        @block.sync
        def _(sp):
            for n in range(RING):
                sp.dma_start(RAW[:, n], wstream[n].rearrange("p (k m) -> p k m", k=4)).then_inc(raw_landed[n], 16)
            with sp.Fori(1, N_UNIT // RING) as i:
                for s in range(RING):
                    sp.wait_ge(lo_ready, (i - 1) * RING + s + 1)
                    sp.dma_start(RAW[:, s], wstream[i * RING + s].rearrange("p (k m) -> p k m", k=4)
                                 ).then_inc(raw_landed[s], 16)
            for k in range(KT // 2):
                sp.wait_ge(out_ready, k + 1)
                sp.dma_start(out[k].rearrange("p (a t) -> p a t", a=2), ACC[:, 2 * k:2 * k + 2]).then_inc(out_stored, 16)
            sp.wait_ge(out_stored, 16 * (KT // 2))

        @block.gpsimd
        def _(pool):
            nc.gpsimd.memset(ONES[:], 1.0).then_inc(ones_set, 1)
            for r in range(2):
                pool.dma_start(XT[:, r], xT[4 * r:4 * r + 4].rearrange("k p t -> p k t")).then_inc(x_landed[r], 16)
                if r == 0:
                    pool.dma_start(GAIN[:], gains.rearrange("p (a k) -> p a k", a=4)).then_inc(small_landed, 16)
                    pool.dma_start(COLS[:], cols).then_inc(small_landed, 16)
            for r in range(2):
                pool.wait_ge(xl_ready, 4 * r + 4)
                pool.wait_ge(xsq_ready, 4 * r + 4)
                pool.dma_start(XT[:, r], xT[8 + 4 * r:12 + 4 * r].rearrange("k p t -> p k t")).then_inc(x_landed[r], 16)
            nc.gpsimd.memset(KTOK[:, 0:P], 0.0)
            nc.gpsimd.memset(VTOK[:, 0], 0.0).then_inc(pads_set, 1)
            for k in range(3):
                pool.dma_start(tmp[k][:], params[k]).then_inc(par_landed, 16)
            pool.dma_start(ROPE[:], consts[:, 0:2 * T].rearrange("p (a t) -> p a t", a=2)).then_inc(consts_landed, 16)
            pool.dma_start(PERM[:], consts[:, 1024:1152]).then_inc(consts_landed, 16)
            pool.dma_start(IDENT[:], consts[:, 1152:1280]).then_inc(consts_landed, 16)
            pool.dma_start(MASK[:], consts[:, 1280:1792].rearrange("p (a t) -> p a t", a=2)).then_inc(consts_landed, 16)
            for r in range(2):
                pool.dma_start(BB[:, :, r], b_pad[r].rearrange("p (c s) -> p c s", c=CT)).then_inc(b_landed, 16)
            pool.dma_start(CST[:], c_pad[0].rearrange("p (q r m) -> p q r m", q=4, r=2)).then_inc(c_landed, 16)

            def store_gate(blk, buf, count):
                pool.wait_ge(gate_ready, count)
                pool.dma_start(gate_dram[blk].rearrange("p (a t) -> p a t", a=2), GS[:, buf]
                               ).then_inc(gate_stored[buf], 16)

            store_gate(0, 0, 1)
            with pool.Fori(1, CT) as c:
                store_gate(c * 2 - 1, 1, c * 2)
                pool.wait_ge(c_done, c * 4)
                pool.dma_start(CST[:], c_pad[c].rearrange("p (q r m) -> p q r m", q=4, r=2)).then_inc(c_landed, 16)
                pool.wait_ge(gate_stored[1], c * 16)
                store_gate(c * 2, 0, c * 2 + 1)
            store_gate(2 * CT - 1, 1, 2 * CT)
            for r in range(2):
                pool.wait_ge(gate_stored[r], 16 * CT)
            pool.wait_ge(y_read, CT)

            def load_gates(p):
                pool.dma_start(GA[:], gate_dram[p].rearrange("p (a t) -> p a t", a=2)).then_inc(ga_landed, 16)
                pool.dma_start(GB[:], gate_dram[p + 8].rearrange("p (a t) -> p a t", a=2)).then_inc(gb_landed, 16)

            load_gates(0)
            with pool.Fori(1, 8) as p:
                pool.wait_ge(bank_read, p * 2 + B_BR)
                load_gates(p)
            pool.wait_ge(unit_done, U_UP)
            for k in range(KT // 2):
                if k >= 2:
                    pool.wait_ge(x1_ready, k - 1)
                pool.dma_start(XR[:, k % 2], xT[2 * k:2 * k + 2].rearrange("k p t -> p k t")).then_inc(xr_landed[k % 2], 16)
                if k >= 1:
                    pool.wait_ge(x1_ready, k)
                    pool.dma_start(x1_dram[k - 1].rearrange("p (a t) -> p a t", a=2), X1[:, (k - 1) % 2]
                                   ).then_inc(x1_stored[(k - 1) % 2], 16)
            pool.wait_ge(x1_ready, KT // 2)
            pool.dma_start(x1_dram[KT // 2 - 1].rearrange("p (a t) -> p a t", a=2), X1[:, 1]).then_inc(x1_stored[1], 16)
            for r in range(2):
                pool.wait_ge(x1_stored[r], 16 * KT // 4)
            pool.wait_ge(unit_done, U_TAIL - 8)
            for k in range(KT // 2):
                pool.dma_start(X1F[:, 2 * k:2 * k + 2], x1_dram[k].rearrange("p (a t) -> p a t", a=2)
                               ).then_inc(x1_back, 16)
            pool.wait_ge(x1_back, 16 * KT // 2)

        @block.scalar
        def _(act):
            def hi(n, s, turns):
                act.wait_ge(raw_landed[s], turns * 16 + 16)
                if not isinstance(n, int) or n >= RING:
                    act.wait_ge(unit_done, n - (RING - 1))
                nc.scalar.activation(WH[:, s], RAW[:, s], ACT.Copy).then_inc(hi_ready, 1)

            def unit(n0, j, i=0, per=0):
                hi(i * per + (n0 + j), (n0 + j) % RING, i * (per // RING) + (n0 + j) // RING)

            act.wait_ge(small_landed, 32)
            for n in range(4):
                if n == 0:
                    unit(0, 0)
                act.wait_ge(x_landed[n % 2], 16 * (n // 2 + 1))
                for k in range(4 * n, 4 * n + 4):
                    nc.scalar.activation(HH[:, k], XT[:, n % 2, k % 4], ACT.Copy,
                                         scale=GAIN[:, 0, k:k + 1]).then_inc(xh_ready, 1)
                    if k >= 2:
                        act.wait_ge(xsum_step, k - 1)
                    nc.scalar.activation(SQX[:, k % 2], XT[:, n % 2, k % 4], ACT.Square).then_inc(xsq_ready, 1)
                unit(n + 1, 0)

            def attention(slot):
                for k in range(4):
                    for a in units_of(slot, N_SLOT0 + 3)[k:k + 1]:
                        act.wait_ge(pv_done, a + 1)
                        n, i = a // 8, a % 8
                        nc.scalar.activation(Q[:, i, n * P:n * P + P], side[:, 3, 0:P], ACT.Copy).then_inc(o_ready, 1)
                    for a in units_of(slot, N_SLOT0 + 2)[k:k + 1]:
                        act.wait_ge(trans_done, a + 1)
                        if a >= 4:
                            act.wait_ge(pv_done, a - 3)
                        nc.scalar.activation(PTB[:, a % 4], side[:, 2], ACT.Copy).then_inc(pt_ready, 1)
                    for a in units_of(slot, N_SLOT0)[k:k + 1]:
                        act.wait_ge(nmax_ready, a + 1)
                        for b in range(2):
                            nc.scalar.activation(PB[:, a % NPB, b], PB[:, a % NPB, b], ACT.Exp,
                                                 bias=SM[:, a % 8, b:b + 1], accum_out=RS[:, a % 8, b:b + 1])
                        nc.scalar.activation(SM[:, a % 8, 2:4], SMK[:, a % 8], ACT.Exp).then_inc(exp_ready, 1)

            for n in range(5, U_GATE):
                unit(n, 0)
                if n == 5:
                    act.wait_ge(stat_done, 1)
                    nc.scalar.activation(STD0[:], side[:, 3], ACT.Sqrt, bias=COLS[:, EPS_C:EPS_C + 1],
                                         scale=1.0 / D).then_inc(std_ready, 1)
                if n == 7:
                    act.wait_ge(angle_ready, 1)
                    nc.scalar.activation(tmp[6][:], tmp[4][:], ACT.Sin)
                    nc.scalar.activation(tmp[7][:], tmp[5][:], ACT.Sin).then_inc(trig_ready, 1)
                if n == 23:
                    act.wait_ge(vt_done, 1)
                    act.wait_ge(pads_set, 1)
                    nc.scalar.activation(VTOK[:, 1:5], side[:, 2].rearrange("p (n d) -> p n d", n=4),
                                         ACT.Copy).then_inc(v_ready, 1)
                if n >= N_SLOT0 + 2:
                    attention(n - 2)

            def stage(c):
                nc.scalar.activation(BST[:], BB[:, c], ACT.Copy)
                nc.scalar.activation(US[:], U[:, c], ACT.Copy).then_inc(stage_ready, 1)

            def sigmoid(count, buf):
                act.wait_ge(bank_read, count + B_GATE)
                nc.scalar.activation(GS[:, buf], GS[:, buf], ACT.Sigmoid).then_inc(gate_ready, 1)

            def gelu(c, count):
                act.wait_ge(y_read, count)
                nc.scalar.activation(U[:, c], U[:, c], ACT.Gelu_apprx_tanh).then_inc(y_ready, 1)

            act.wait_ge(bb_ready, 1)
            for j in range(8):
                unit(U_GATE, j)
                if j == 0:
                    attention(U_GATE - 2)
                    act.wait_ge(o_ready, 32)
                    act.wait_ge(bank_read, 6)
                    stage(0)
                if j == 5:
                    sigmoid(1, 0)
            with act.Fori(1, CT) as c:
                for j in range(8):
                    unit(U_GATE, j, c, 8)
                    if j == 0:
                        act.wait_ge(bu_done, c * 4)
                        stage(c)
                    if j == 1:
                        sigmoid(c * 2, 1)
                    if j == 4:
                        gelu(c - 1, c)
                    if j == 5:
                        sigmoid(c * 2 + 1, 0)
            unit(U_GLU, 0)
            unit(U_GLU, 1)
            sigmoid(2 * CT, 1)

            def y_hi(c):
                nc.scalar.activation(YH[:, c], U[:, c], ACT.Copy).then_inc(yh_ready, 1)

            act.wait_ge(unit_done, U_GLU)
            act.wait_ge(y_ready, CT - 1)
            for c in range(CT - 1):
                y_hi(c)
            gelu(CT - 1, CT)
            act.wait_ge(y_ready, CT)
            y_hi(CT - 1)

            def glu(b, part):
                if part == 0:
                    act.wait_ge(unit_done, U_GLU + 2 * b + 2)
                    act.wait_ge(bank_read, B_GLU + b)
                    nc.scalar.activation(SG[:], main[:, 2 * ((B_GLU + b) % 2) + 1], ACT.Sigmoid).then_inc(sig_ready, 1)
                else:
                    act.wait_ge(bank_read, B_GLU + b + 1)
                    nc.scalar.activation(OSH[:, b], OT[:], ACT.Copy).then_inc(osh_ready, 1)

            for j in range(2, 16):
                unit(U_GLU, j)
                if j == 2:
                    for r in range(2):
                        act.wait_ge(gate_stored[r], 16 * CT)
                    for k in range(CT):
                        nc.scalar.activation(OAH[:, k], Q[:, k], ACT.Copy).then_inc(oah_ready, 1)
                if j % 2 == 1:
                    glu((j - 3) // 2, 0)
                    glu((j - 3) // 2, 1)

            def branch(p, count):
                act.wait_ge(br_ready, count)
                nc.scalar.activation(MH[:, bass.ds(p * 2, 2)], TB[:], ACT.Copy).then_inc(mh_ready, 1)

            for j in range(4):
                unit(U_BR, j)
                if j == 1:
                    glu(7, 0)
                    glu(7, 1)
            with act.Fori(1, 8) as p:
                for j in range(4):
                    unit(U_BR, j, p, 4)
                    if j == 1:
                        branch(p - 1, p)

            def squares(count):
                act.wait_ge(bank_read, count)
                act.wait_ge(sq_used, count - B_OUT)
                nc.scalar.activation(SQ[:, 0], Z[:, bass.ds((count - B_OUT - 1) * 2, 2)], ACT.Square).then_inc(sq_ready, 1)

            for j in range(8):
                unit(U_OUT, j)
                if j == 1:
                    branch(7, 8)
                if j == 5:
                    squares(B_OUT + 1)
            with act.Fori(1, 4) as i:
                for j in range(8):
                    unit(U_OUT, j, i, 8)
                    if j == 1:
                        squares(i * 2 + B_OUT)
                    if j == 5:
                        squares(i * 2 + B_OUT + 1)
            unit(U_UP, 0)
            unit(U_UP, 1)
            squares(B_UP)
            act.wait_ge(stat_done, 2)
            nc.scalar.activation(RSTD[:], side[:, 3], ACT.Sqrt, bias=COLS[:, EPS_C:EPS_C + 1],
                                 scale=1.0 / D).then_inc(std_ready, 1)
            for k in range(KT // 2):
                act.wait_ge(x1_ready, k + 1)
                for t in range(2):
                    ins = nc.scalar.activation(MH[:, 2 * k + t], X1[:, k % 2, t], ACT.Copy,
                                               scale=GAIN[:, 2, 2 * k + t:2 * k + t + 1])
                ins.then_inc(h2h_ready, 1)
                if k >= 2:
                    act.wait_ge(h2sq_used, k - 1)
                nc.scalar.activation(SQ[:, k % 2], X1[:, k % 2], ACT.Square).then_inc(h2sq_ready, 1)
                if k % 2 == 1:
                    if k // 2 < 2:
                        unit(U_UP, 2 + k // 2)
            for j in range(4, 8):
                unit(U_UP, j)
                if j == 5:
                    act.wait_ge(stat_done, 3)
                    nc.scalar.activation(RSTD[:], side[:, 2], ACT.Sqrt, bias=COLS[:, EPS_C:EPS_C + 1],
                                         scale=1.0 / D).then_inc(std_ready, 1)
                    act.wait_ge(a_ready, 1)
                    nc.scalar.activation(AH[:, 0, 0:2], AA[:], ACT.Copy).then_inc(ah_ready, 1)

            def a_hi(buf, half, count):
                act.wait_ge(a_ready, count)
                nc.scalar.activation(AH[:, buf, 2 * half:2 * half + 2], AA[:], ACT.Copy).then_inc(ah_ready, 1)

            for j in range(16):
                unit(U_MLP, j)
                if j == 1:
                    a_hi(0, 1, 2)
                if j == 5:
                    a_hi(1, 0, 3)
                if j == 9:
                    a_hi(1, 1, 4)
            with act.Fori(0, (N_GROUP - 2) // 2) as i:
                for j in range(32):
                    unit(U_MLP + 16, j, i, 32)
                    if j % 16 == 5:
                        a_hi(j // 16, 0, i * 4 + (5 + 2 * (j // 16)))
                    if j % 16 == 9:
                        a_hi(j // 16, 1, i * 4 + (6 + 2 * (j // 16)))

            def final_squares(m):
                act.wait_ge(bank_read, B_TAIL + m + 1)
                act.wait_ge(fsq_used, m + 1)
                nc.scalar.activation(SQ[:, 0], ACC[:, 2 * m:2 * m + 2], ACT.Square).then_inc(fsq_ready, 1)

            for j in range(8):
                unit(U_TAIL, j)
                if j >= 3:
                    final_squares(j - 3)
            for m in range(5, 8):
                final_squares(m)
            act.wait_ge(stat_done, 4)
            nc.scalar.activation(RSTD[:], side[:, 3], ACT.Sqrt, bias=COLS[:, EPS_C:EPS_C + 1],
                                 scale=1.0 / D).then_inc(std_ready, 1)

        @block.vector
        def _(v):
            step = Count(dve_step)

            def link(ins):
                ins.then_inc(dve_step, 1)
                step.n += 1
                v.wait_ge(dve_step, step.value())

            def link_to(ins, sem_, value):
                ins.then_inc(sem_, 1)
                v.wait_ge(sem_, value)

            tt, stt, ts = nc.vector.tensor_tensor, nc.vector.scalar_tensor_tensor, nc.vector.tensor_scalar

            def lo(n, s):
                v.wait_ge(hi_ready, n + 1)
                tt(WL[:, s], RAW[:, s], WH[:, s].bitcast(F32), ALU.subtract).then_inc(lo_ready, 1)

            def unit(n0, j, i=0, per=0):
                lo(i * per + (n0 + j), (n0 + j) % RING)

            def pair(b):
                return main[:, 2 * (b % 2):2 * (b % 2) + 2]

            def both(ap):
                return ap.unsqueeze(1).to_broadcast([P, 2, T])

            link_to(nc.vector.memset(SUM0[:], 0.0), rope_free, 1)
            v.wait_ge(small_landed, 32)
            for n in range(4):
                if n == 0:
                    unit(0, 0)
                for k in range(4 * n, 4 * n + 4):
                    v.wait_ge(xh_ready, k + 1)
                    stt(out=HL[:, k], in0=XT[:, n % 2, k % 4], scalar=GAIN[:, 0, k:k + 1],
                        in1=HH[:, k].bitcast(F32), op0=ALU.mult, op1=ALU.subtract).then_inc(xl_ready, 1)
                    v.wait_ge(xsq_ready, k + 1)
                    link_to(tt(SUM0[:], SUM0[:], SQX[:, k % 2], ALU.add), xsum_step, k + 1)
                unit(n + 1, 0)

            def exp(out_, x, k, r, q):
                link(ts(out_, x, -87.336, None, ALU.is_ge))
                link(ts(x, x, -87.336, 88.37, ALU.max, ALU.min))
                link(ts(k, x, LOG2E, MAGIC, ALU.mult, ALU.add))
                link(ts(k, k, -MAGIC, None, ALU.add))
                link(stt(out=r, in0=k, scalar=-LN2_HI, in1=x, op0=ALU.mult, op1=ALU.add))
                link(stt(out=r, in0=k, scalar=-LN2_LO, in1=r, op0=ALU.mult, op1=ALU.add))
                link(ts(q, r, EXP_COEF[0], None, ALU.mult))
                for coef in EXP_COEF[1:]:
                    link(stt(out=q, in0=q, scalar=coef, in1=r, op0=ALU.add, op1=ALU.mult))
                link(stt(out=out_, in0=q, scalar=1.0, in1=out_, op0=ALU.add, op1=ALU.mult))
                link(ts(r.bitcast(I32), k, 127.0, 8388608.0, ALU.add, ALU.mult))
                link(tt(out_, out_, r, ALU.mult))

            A = [x[:] for x in tmp]

            def time_step():
                v.wait_ge(par_landed, 48)
                exp(A[3], A[2], A[8], A[9], A[10])

            def angles():
                link(tt(A[4], A[1], A[3], ALU.mult))
                link(tt(A[2], A[0], A[3], ALU.mult))
                link(ts(A[8], A[4], 1.0 / (2 * np.pi), MAGIC, ALU.mult, ALU.add))
                link(ts(A[8], A[8], -MAGIC, None, ALU.add))
                for part in TWO_PI:
                    link(stt(out=A[4], in0=A[8], scalar=-part, in1=A[4], op0=ALU.mult, op1=ALU.add))
                link(ts(A[4], A[4], -PI_SAFE, PI_SAFE, ALU.max, ALU.min))
                link(stt(out=A[5], in0=A[4], scalar=-1.0, in1=A[4], op0=ALU.mult, op1=ALU.max))
                link_to(ts(A[5], A[5], -1.0, float(np.pi / 2), ALU.mult, ALU.add), angle_ready, 1)

            def decay():
                exp(A[3], A[2], A[8], A[9], A[10])
                link(nc.vector.tensor_copy(MAG[:], A[3][:, NW:NP]))

            def coefficients():
                v.wait_ge(trig_ready, 1)
                w = slice(0, NW)
                link(nc.vector.tensor_copy(PW[:, 0, 0], A[7][:, NW:NP]))
                link(nc.vector.tensor_copy(PW[:, 0, 1], A[6][:, NW:NP]))
                link(tt(A[7][:, w], A[7][:, w], A[3][:, w], ALU.mult))
                link(tt(A[6][:, w], A[6][:, w], A[3][:, w], ALU.mult))
                link(ts(A[7][:, w], A[7][:, w], -1.0, None, ALU.add))
                link(tt(A[8][:, w], A[0][:, w], A[0][:, w], ALU.mult))
                link(tt(A[9][:, w], A[1][:, w], A[1][:, w], ALU.mult))
                link(tt(A[8][:, w], A[8][:, w], A[9][:, w], ALU.add))
                link(nc.vector.reciprocal(A[8][:, w], A[8][:, w]))
                link(tt(A[2][:, w], A[7][:, w], A[0][:, w], ALU.mult))
                link(tt(A[9][:, w], A[6][:, w], A[1][:, w], ALU.mult))
                link(tt(A[2][:, w], A[2][:, w], A[9][:, w], ALU.add))
                link(tt(A[2][:, w], A[2][:, w], A[8][:, w], ALU.mult))
                link(tt(A[10][:, w], A[6][:, w], A[0][:, w], ALU.mult))
                link(tt(A[9][:, w], A[7][:, w], A[1][:, w], ALU.mult))
                link(tt(A[10][:, w], A[10][:, w], A[9][:, w], ALU.subtract))
                link(tt(A[10][:, w], A[10][:, w], A[8][:, w], ALU.mult))

            def b_bar():
                v.wait_ge(b_landed, 32)

                def spread(x):
                    return x[:, 0:NW].rearrange("p (c s) -> p c s", c=CT).unsqueeze(2).to_broadcast([P, CT, 2, SSM_S])

                def halves(x):
                    return x.rearrange("p c (g s) -> p c g s", g=2)

                br, bi = halves(BB[:, :, 0]), halves(BB[:, :, 1])
                t1, t2 = halves(BT[0][:]), halves(BT[1][:])
                cr, ci = spread(A[2]), spread(A[10])
                link(tt(t1, bi, ci, ALU.mult))
                link(tt(t2, br, ci, ALU.mult))
                link(tt(br, br, cr, ALU.mult))
                link(tt(br, br, t1, ALU.subtract))
                link(tt(bi, bi, cr, ALU.mult))
                link_to(tt(bi, bi, t2, ALU.add), bb_ready, 1)

            def powers():
                t1, t2 = A[8][:, 0:ST], A[9][:, 0:ST]
                for k in range(1, NPOW):
                    c_, s_ = PW[:, k - 1, 0], PW[:, k - 1, 1]
                    tt(t1, c_, c_, ALU.mult)
                    link(tt(t2, s_, s_, ALU.mult))
                    tt(PW[:, k, 0], t1, t2, ALU.subtract)
                    link(stt(out=PW[:, k, 1], in0=c_, scalar=2.0, in1=s_, op0=ALU.mult, op1=ALU.mult))

            def rotation_start():
                link(nc.vector.memset(E32[:, :, 0, 0:1], 1.0))
                link(nc.vector.memset(E32[:, :, 1, 0:1], 0.0))
                for k in range(5):
                    n = 1 << k
                    t1 = A[8][:, 0:ST * n].rearrange("p (s j) -> p s j", s=ST)
                    t2 = A[9][:, 0:ST * n].rearrange("p (s j) -> p s j", s=ST)
                    er, ei = E32[:, :, 0, 0:n], E32[:, :, 1, 0:n]
                    pr = PW[:, k, 0].unsqueeze(2).to_broadcast([P, ST, n])
                    pi = PW[:, k, 1].unsqueeze(2).to_broadcast([P, ST, n])
                    tt(t1, er, pr, ALU.mult)
                    link(tt(t2, ei, pi, ALU.mult))
                    link(tt(E32[:, :, 0, n:2 * n], t1, t2, ALU.subtract))
                    tt(t1, er, pi, ALU.mult)
                    link(tt(t2, ei, pr, ALU.mult))
                    link(tt(E32[:, :, 1, n:2 * n], t1, t2, ALU.add))

            def normed(out_, b):
                v.wait_ge(unit_done, UNIT_END[b])
                link_to(tt(out_, pair(b), both(RSTD[:]), ALU.mult), bank_read, b + 1)

            def rope(x, b):
                w = x.shape[1]
                v.wait_ge(rope_mm, b + 1)
                v.wait_ge(consts_landed, 64)
                t = KV[:, 0] if w == 1 else KV[:]
                xx = x[:, 0] if w == 1 else x
                psum = side[:, 0] if w == 1 else side[:, 0:2]
                cos_ = ROPE[:, 0] if w == 1 else both(ROPE[:, 0])
                sin_ = ROPE[:, 1] if w == 1 else both(ROPE[:, 1])
                return xx, t, psum, cos_, sin_

            def rope_q(b):
                xx, t, psum, cos_, sin_ = rope(Q[:, 2 * b:2 * b + 2], b)
                link(tt(t, psum, sin_, ALU.mult))
                link(tt(xx, xx, cos_, ALU.mult))
                link_to(tt(xx, xx, t, ALU.add), rope_free, b + 2)

            def rope_k():
                v.wait_ge(rope_mm, 5)
                v.wait_ge(vt_done, 1)
                v.wait_ge(pads_set, 1)
                link(tt(KV[:, 1], side[:, 0], ROPE[:, 1], ALU.mult))
                link(tt(KV[:, 0], KV[:, 0], ROPE[:, 0], ALU.mult))
                link_to(tt(KTOK[:, P:P + T], KV[:, 0], KV[:, 1], ALU.add), rope_free, 6)

            UNIT_END = {b: 4 * b + 4 for b in range(9)}

            def normalise(a):
                v.wait_ge(exp_ready, a + 1)
                link(tt(RS[:, a % 8], RS[:, a % 8], SM[:, a % 8, 2:4], ALU.add))
                link(nc.vector.reciprocal(RS[:, a % 8], RS[:, a % 8]))
                ts(PB[:, a % NPB, 0], PB[:, a % NPB, 0], RS[:, a % 8, 0:1], None, ALU.mult)
                link_to(ts(PB[:, a % NPB, 1], PB[:, a % NPB, 1], RS[:, a % 8, 1:2], None, ALU.mult),
                        probs_ready, a + 1)

            def mask_and_max(a):
                n, i = a // 8, a % 8
                v.wait_ge(scores_done, a + 1)
                if a >= NPB:
                    v.wait_ge(trans_done, a - NPB + 1)
                mask = MASK[:, 0 if n == 0 else 1].unsqueeze(1).to_broadcast([P, 2, 256])
                link_to(stt(out=PB[:, a % NPB], in0=side[:, 0:2, 0:256], scalar=HEAD ** -0.5, in1=mask,
                            op0=ALU.mult, op1=ALU.min), scores_read, a + 1)
                link(nc.vector.reduce_max(MX[:, a % 8], PB[:, a % NPB], AX))
                link(tt(MX[:, a % 8], MX[:, a % 8], COLS[:, SINK + 2 * i:SINK + 2 * i + 2], ALU.max))
                link(tt(SMK[:, a % 8], COLS[:, SINK + 2 * i:SINK + 2 * i + 2], MX[:, a % 8], ALU.subtract))
                link_to(ts(SM[:, a % 8, 0:2], MX[:, a % 8], -1.0, None, ALU.mult), nmax_ready, a + 1)

            def attention(slot):
                for a in units_of(slot, N_SLOT0):
                    if a >= 1:
                        normalise(a - 1)
                    mask_and_max(a)
                if slot == N_SLOT0 + 8:
                    normalise(31)

            params_at = {4: time_step, 6: angles, 8: decay, 10: coefficients, 12: b_bar, 14: powers, 16: rotation_start}
            for n in range(4, U_GATE):
                if n > 4:
                    unit(n, 0)
                if n in params_at:
                    params_at[n]()
                if n == 5:
                    v.wait_ge(std_ready, 1)
                    link(nc.vector.reciprocal(RSTD[:], STD0[:]))
                if n % 4 == 1 and n <= 17:
                    b = (n - 5) // 4
                    normed(Q[:, 2 * b:2 * b + 2], b)
                if n % 4 == 3 and 7 <= n <= 19:
                    rope_q((n - 7) // 4)
                if n == 21:
                    normed(KV[:], 4)
                if n == 23:
                    rope_k()
                if n in (25, 29, 33):
                    b = (n - 5) // 4
                    normed(U[:, 2 * b - 10:2 * b - 8], b)
                if n >= N_SLOT0 + 2:
                    attention(n - 2)

            def scan_tile(c, q):
                s = c * 4 + q
                col = bass.ds(s, 1)
                link(nc.vector.tensor_copy(ROT_T[:, :, 0:EJ], E32[:, col].squeeze(1) if isinstance(s, int) else E32[:, s]))
                n = EJ
                for k in range(5, NPOW):
                    pr, pi = PW[:, k, 0, col], PW[:, k, 1, col]
                    link(ts(M1[:, :, 0:n], ROT_T[:, :, 0:n], pi, None, ALU.mult))
                    stt(out=ROT_T[:, 0, n:2 * n], in0=ROT_T[:, 0, 0:n], scalar=pr, in1=M1[:, 1, 0:n],
                        op0=ALU.mult, op1=ALU.subtract)
                    link(stt(out=ROT_T[:, 1, n:2 * n], in0=ROT_T[:, 1, 0:n], scalar=pr, in1=M1[:, 0, 0:n],
                             op0=ALU.mult, op1=ALU.add))
                    n *= 2
                cos_, sin_ = both(ROT_T[:, 0]), both(ROT_T[:, 1])
                v.wait_ge(bu_done, s + 1)
                tt(M1[:], side[:, 0:2], cos_, ALU.mult)
                link_to(tt(M2[:], side[:, 0:2], sin_, ALU.mult), bu_read, s + 1)
                tt(WI[:, 0], M1[:, 0], M2[:, 1], ALU.add)
                link(tt(WI[:, 1], M1[:, 1], M2[:, 0], ALU.subtract))
                r = MAG[:, col].to_broadcast([P, T])
                nc.vector.tensor_tensor_scan(WO[:, 0], r, WI[:, 0], 0.0, ALU.mult, ALU.add)
                link(nc.vector.tensor_tensor_scan(WO[:, 1], r, WI[:, 1], 0.0, ALU.mult, ALU.add))
                tt(M1[:], WO[:], cos_, ALU.mult)
                link(tt(M2[:], WO[:], sin_, ALU.mult))
                if not isinstance(s, int) or s >= 2:
                    v.wait_ge(c_done, s - 1)
                tt(SB[:, q % 2, 0], M1[:, 0], M2[:, 1], ALU.subtract)
                link_to(stt(out=SB[:, q % 2, 1], in0=M1[:, 1], scalar=-1.0, in1=M2[:, 0],
                            op0=ALU.mult, op1=ALU.subtract), state_ready, s + 1)

            def gate(buf, b, end):
                v.wait_ge(unit_done, end)
                link_to(tt(GS[:, buf], main[:, 2 - 2 * buf:4 - 2 * buf], both(RSTD[:]), ALU.mult), bank_read, b + 1)

            def y_out(c, count):
                v.wait_ge(c_done, count * 4)
                v.wait_ge(stage_ready, count)
                link_to(stt(out=U[:, c], in0=U[:, c], scalar=COLS[:, bass.ds(c + D_SKIP, 1)], in1=side[:, 2],
                            op0=ALU.mult, op1=ALU.add), y_read, count)

            for j in range(8):
                unit(U_GATE, j)
                if j == 0:
                    attention(U_GATE - 2)
                if j == 1:
                    normed(U[:, 6:8], 8)
                if j >= 2 and j % 2 == 0:
                    if j == 2:
                        v.wait_ge(o_ready, 32)
                    scan_tile(0, j // 2 - 1)
                if j == 5:
                    gate(0, B_GATE, U_GATE + 4)
            per = 4 * (4 + 2 * (NPOW - 5))
            with v.Fori(1, CT) as c:
                step.enter(c, 1, per)
                for j in range(8):
                    unit(U_GATE, j, c, 8)
                    if j == 0:
                        scan_tile(c - 1, 3)
                    if j == 1:
                        v.wait_ge(gate_stored[0], c * 16)
                        gate(1, c * 2 + (B_GATE - 1), c * 8 + U_GATE)
                    if j == 4:
                        y_out(c - 1, c)
                    if j >= 2 and j % 2 == 0:
                        scan_tile(c, j // 2 - 1)
                    if j == 5:
                        v.wait_ge(gate_stored[0], c * 16)
                        gate(0, c * 2 + B_GATE, c * 8 + (U_GATE + 4))
                step.leave(1, CT)
            scan_tile(CT - 1, 3)
            unit(U_GLU, 0)
            v.wait_ge(gate_stored[1], 16 * (CT - 1))
            gate(1, B_GLU - 1, U_GLU)
            unit(U_GLU, 1)

            def y_lo(c):
                v.wait_ge(yh_ready, c + 1)
                tt(YL[:, c], U[:, c], YH[:, c].bitcast(F32), ALU.subtract).then_inc(yl_ready, 1)

            y_out(CT - 1, CT)
            for c in range(CT):
                y_lo(c)

            def glu(b):
                v.wait_ge(sig_ready, b + 1)
                if b >= 1:
                    v.wait_ge(osh_ready, b)
                link_to(tt(OT[:], main[:, 2 * ((B_GLU + b) % 2)], SG[:], ALU.mult), bank_read, B_GLU + b + 1)

            def glu_lo(b):
                v.wait_ge(osh_ready, b + 1)
                link_to(tt(OSL[:, b], OT[:], OSH[:, b].bitcast(F32), ALU.subtract), osl_ready, b + 1)

            for j in range(2, 16):
                unit(U_GLU, j)
                if j == 3:
                    glu(0)
                if j % 2 == 0 and j >= 4:
                    glu_lo((j - 4) // 2)
                if j % 2 == 1 and j >= 5:
                    glu((j - 3) // 2)
                if j in (4, 6):
                    for k in range(2 * j - 8, 2 * j - 4):
                        v.wait_ge(oah_ready, k + 1)
                        tt(OAL[:, k], Q[:, k], OAH[:, k].bitcast(F32), ALU.subtract).then_inc(oal_ready, 1)

            def branch_attn(p, b, end):
                v.wait_ge(unit_done, end)
                v.wait_ge(ga_landed, p * 16 + 16)
                link_to(tt(TA[:], main[:, 2:4], GA[:], ALU.mult), bank_read, b + 1)

            def branch_ssm(p, b, end):
                v.wait_ge(unit_done, end)
                v.wait_ge(gb_landed, p * 16 + 16)
                link_to(tt(TB[:], main[:, 0:2], GB[:], ALU.mult), bank_read, b + 1)
                link_to(tt(TB[:], TB[:], TA[:], ALU.add), br_ready, p + 1)

            def branch_lo(p):
                v.wait_ge(mh_ready, p + 1)
                t = bass.ds(p * 2, 2)
                link_to(tt(ML[:, t], TB[:], MH[:, t].bitcast(F32), ALU.subtract), ml_ready, p + 1)

            for j in range(4):
                unit(U_BR, j)
                if j == 0:
                    glu_lo(6)
                if j == 1:
                    glu(7)
                if j == 2:
                    glu_lo(7)
                if j == 3:
                    branch_attn(0, B_BR, U_BR + 2)
            with v.Fori(1, 8) as p:
                for j in range(4):
                    unit(U_BR, j, p, 4)
                    if j == 1:
                        branch_ssm(p - 1, p * 2 + (B_BR - 1), p * 4 + U_BR)
                    if j == 2:
                        branch_lo(p - 1)
                    if j == 3:
                        branch_attn(p, p * 2 + B_BR, p * 4 + (U_BR + 2))

            def mixed(i, b, end, buf):
                v.wait_ge(unit_done, end)
                link_to(nc.vector.tensor_copy(Z[:, bass.ds(i * 2, 2)], main[:, buf:buf + 2]), bank_read, b + 1)

            def add_squares(count):
                v.wait_ge(sq_ready, count)
                link_to(tt(SQS[:], SQS[:], SQ[:, 0], ALU.add), sq_used, count + 1)

            for j in range(8):
                unit(U_OUT, j)
                if j == 1:
                    branch_ssm(7, B_OUT - 1, U_OUT)
                if j == 2:
                    branch_lo(7)
                if j == 3:
                    link_to(nc.vector.memset(SQS[:], 0.0), sq_used, 1)
                if j == 5:
                    mixed(0, B_OUT, U_OUT + 4, 2)
                if j == 6:
                    add_squares(1)
            with v.Fori(1, 4) as i:
                for j in range(8):
                    unit(U_OUT, j, i, 8)
                    if j == 1:
                        mixed(i * 2 - 1, i * 2 + (B_OUT - 1), i * 8 + U_OUT, 0)
                    if j == 2:
                        add_squares(i * 2)
                    if j == 5:
                        mixed(i * 2, i * 2 + B_OUT, i * 8 + (U_OUT + 4), 2)
                    if j == 6:
                        add_squares(i * 2 + 1)
            unit(U_UP, 0)
            unit(U_UP, 1)
            mixed(7, B_UP - 1, U_UP, 0)
            add_squares(8)
            link_to(tt(SQS[:, 0], SQS[:, 0], SQS[:, 1], ALU.add), sum_ready, 1)
            v.wait_ge(std_ready, 2)
            link(nc.vector.reciprocal(RSTD[:], RSTD[:]))

            def h2_lo(k):
                v.wait_ge(h2h_ready, k + 1)
                for t in (2 * k, 2 * k + 1):
                    ins = stt(out=ML[:, t], in0=X1[:, k % 2, t % 2], scalar=GAIN[:, 2, t:t + 1],
                              in1=MH[:, t].bitcast(F32), op0=ALU.mult, op1=ALU.subtract)
                link_to(ins, h2l_ready, k + 1)

            for k in range(KT // 2):
                v.wait_ge(xr_landed[k % 2], 16 * (k // 2 + 1))
                if k >= 2:
                    v.wait_ge(x1_stored[k % 2], 16 * (k // 2))
                    v.wait_ge(h2sq_ready, k - 1)
                for t in range(2):
                    ins = stt(out=X1[:, k % 2, t], in0=Z[:, 2 * k + t], scalar=GAIN[:, 1, 2 * k + t:2 * k + t + 1],
                              in1=RSTD[:], op0=ALU.mult, op1=ALU.mult)
                link(ins)
                link_to(tt(X1[:, k % 2], X1[:, k % 2], XR[:, k % 2], ALU.add), x1_ready, k + 1)
                if k >= 1:
                    h2_lo(k - 1)
                if k % 2 == 1 and k // 2 < 2:
                    unit(U_UP, 2 + k // 2)
            h2_lo(KT // 2 - 1)

            def up(b, end, buf, count):
                v.wait_ge(unit_done, end)
                link_to(tt(TT[:], main[:, buf:buf + 2], both(RSTD[:]), ALU.mult), bank_read, b + 1)
                link_to(stt(out=AA[:], in0=TT[:], scalar=0.0, in1=TT[:], op0=ALU.max, op1=ALU.mult), a_ready, count)

            def up_lo(buf, half, count):
                v.wait_ge(ah_ready, count)
                link_to(tt(AL[:, buf, 2 * half:2 * half + 2], AA[:], AH[:, buf, 2 * half:2 * half + 2].bitcast(F32),
                           ALU.subtract), al_ready, count)

            def down(m, b, end, first=False):
                v.wait_ge(unit_done, end)
                o, ps = ACC[:, 2 * m:2 * m + 2], main[:, 2 - 2 * (m % 2):4 - 2 * (m % 2)]
                if first:
                    link_to(nc.vector.tensor_copy(o, ps), bank_read, b + 1)
                else:
                    link_to(tt(o, ps, o, ALU.add), bank_read, b + 1)

            for j in range(4, 8):
                unit(U_UP, j)
                if j == 5:
                    v.wait_ge(std_ready, 3)
                    link(nc.vector.reciprocal(RSTD[:], RSTD[:]))
                    for r in range(2):
                        v.wait_ge(x1_stored[r], 16 * KT // 4)
                    up(B_UP, U_UP + 4, 2, 1)
                if j == 6:
                    up_lo(0, 0, 1)

            def group(j, buf, n0, b0, counts, first):
                if not first and j < 2:
                    down(6 + j, b0 - 2 + j, n0 - 1 + j)
                if j == 5 or j == 9:
                    h = j // 4 - 1
                    up(b0 + h, n0 + 4 + 4 * h, 2 - 2 * h, counts + h + 1)
                if j == 6 or j == 10:
                    h = j // 4 - 1
                    up_lo(buf, h, counts + h + 1)
                if j >= 10:
                    down(j - 10, b0 + (j - 8), n0 + (j - 1), first)

            for j in range(16):
                unit(U_MLP, j)
                if j == 1:
                    up(B_UP + 1, U_UP + 8, 0, 2)
                if j == 2:
                    up_lo(0, 1, 2)
                if j == 3:
                    link(nc.vector.memset(ACC[:, 12:16], 0.0))
                group(j, 1, U_MLP, B_MLP, 2, True)
            with v.Fori(0, (N_GROUP - 2) // 2) as i:
                for j in range(32):
                    unit(U_MLP + 16, j, i, 32)
                    h = j // 16
                    group(j % 16, h, i * 32 + (U_MLP + 16 + 16 * h), i * 20 + (B_MLP + 10 + 10 * h),
                          i * 4 + (4 + 2 * h), False)

            def add_final(m):
                v.wait_ge(fsq_ready, m + 1)
                link_to(tt(SQS[:], SQS[:], SQ[:, 0], ALU.add), fsq_used, m + 2)

            for j in range(8):
                unit(U_TAIL, j)
                if j < 2:
                    down(6 + j, B_TAIL - 2 + j, U_TAIL - 1 + j)
                else:
                    down(j - 2, B_TAIL + j - 2, U_TAIL + j - 1)
                if j == 2:
                    link_to(nc.vector.memset(SQS[:], 0.0), fsq_used, 1)
                if j >= 4:
                    add_final(j - 4)
            for m in (6, 7):
                down(m, B_TAIL + m, U_TAIL + m + 1)
            for m in range(4, 8):
                add_final(m)
            link_to(tt(SQS[:, 0], SQS[:, 0], SQS[:, 1], ALU.add), sum_ready, 2)
            v.wait_ge(std_ready, 4)
            link(nc.vector.reciprocal(RSTD[:], RSTD[:]))
            v.wait_ge(x1_back, 16 * KT // 2)
            for k in range(KT // 2):
                for t in range(2 * k, 2 * k + 2):
                    ins = stt(out=ACC[:, t], in0=ACC[:, t], scalar=GAIN[:, 3, t:t + 1], in1=RSTD[:],
                              op0=ALU.mult, op1=ALU.mult)
                link(ins)
                tt(ACC[:, 2 * k:2 * k + 2], ACC[:, 2 * k:2 * k + 2], X1F[:, 2 * k:2 * k + 2], ALU.add).then_inc(out_ready, 1)

        @block.tensor
        def _(pe):
            mm = nc.tensor.matmul

            def product(n, s, b_odd, xh, xl, k0, first, last):
                pe.wait_ge(lo_ready, n + 1)
                for k in range(4):
                    for m in range(2):
                        wh, wl = WH[:, s, k, m * P:m * P + P], WL[:, s, k, m * P:m * P + P]
                        o = main[:, 2 * b_odd + m]
                        mm(o, wh, xh[:, k0 + k], start=first and k == 0, stop=False)
                        mm(o, wh, xl[:, k0 + k], start=False, stop=False)
                        ins = mm(o, wl, xh[:, k0 + k], start=False, stop=last and k == 3)
                ins.then_inc(unit_done, 1)

            def take_bank(b):
                if not isinstance(b, int) or b >= 2:
                    pe.wait_ge(bank_read, b - 1)

            for n in range(4):
                pe.wait_ge(xl_ready, 4 * n + 4)
                product(n, n, 0, HH, HL, 4 * n, n == 0, n == 3)
            pe.wait_ge(ones_set, 1)
            pe.wait_ge(xsum_step, KT)
            mm(side[:, 3], ONES[:], SUM0[:], start=True, stop=True).then_inc(stat_done, 1)

            def rope(x, b, tiles):
                pe.wait_ge(bank_read, b + 1)
                pe.wait_ge(rope_free, b + 1)
                for t in range(tiles):
                    ins = mm(side[:, t], PERM[:], x(t), start=True, stop=True)
                ins.then_inc(rope_mm, 1)

            pe.wait_ge(consts_landed, 64)
            with pe.Fori(0, 2) as i:
                for j in range(8):
                    if j % 4 == 0:
                        take_bank(i * 2 + (1 + j // 4))
                    product(i * 8 + (4 + j), j % 4, 1 - j // 4, HH, HL, 4 * (j % 4), j % 4 == 0, j % 4 == 3)
                    if j in (1, 5):
                        h = j // 4
                        rope(lambda t: Q[:, i * 4 + (2 * h + t)], i * 2 + h, 2)

            def attention(slot):
                for k in range(4):
                    for a in units_of(slot, N_SLOT0 + 3)[k:k + 1]:
                        n, i = a // 8, a % 8
                        pe.wait_ge(pt_ready, a + 1)
                        if a >= 1:
                            pe.wait_ge(o_ready, a)
                        for b in range(2):
                            for kb in range(2):
                                ins = mm(side[HEAD * b:HEAD * b + HEAD, 3, 0:P],
                                         VTOK[:, n + kb, HEAD * b:HEAD * b + HEAD],
                                         PTB[:, a % 4, (2 * b + kb) * P:(2 * b + kb + 1) * P],
                                         start=kb == 0, stop=kb == 1)
                        ins.then_inc(pv_done, 1)
                    for a in units_of(slot, N_SLOT0)[k:k + 1]:
                        n, i = a // 8, a % 8
                        if a >= 1:
                            pe.wait_ge(scores_read, a)
                        for b in range(2):
                            r = slice(HEAD * b, HEAD * b + HEAD)
                            ins = mm(side[:, b, 0:256], Q[r, i, n * P:n * P + P], KTOK[r, n * P:n * P + 2 * P],
                                     start=True, stop=True)
                        ins.then_inc(scores_done, 1)
                    for a in units_of(slot, N_SLOT0 + 2)[k:k + 1]:
                        pe.wait_ge(probs_ready, a + 1)
                        if a >= 1:
                            pe.wait_ge(pt_ready, a)
                        for b in range(2):
                            for kb in range(2):
                                ins = nc.tensor.transpose(side[:, 2, (2 * b + kb) * P:(2 * b + kb + 1) * P],
                                                          PB[:, a % NPB, b, kb * P:kb * P + P], IDENT[:])
                        ins.then_inc(trans_done, 1)

            for n in range(U_U, U_GATE):
                b, j = 5 + (n - U_U) // 4, (n - U_U) % 4
                if j == 0:
                    take_bank(b)
                product(n, n % 4, b % 2, HH, HL, 4 * j, j == 0, j == 3)
                if n == 21:
                    rope(lambda t: KV[:, 0], 4, 1)
                    for t in range(4):
                        ins = nc.tensor.transpose(side[:, 2, t * P:t * P + P], KV[:, 1, t * P:t * P + P], IDENT[:])
                    ins.then_inc(vt_done, 1)
                if n == N_SLOT0:
                    pe.wait_ge(rope_free, 6)
                    pe.wait_ge(v_ready, 1)
                if n >= N_SLOT0:
                    attention(n)

            def bu(c, q):
                s = c * 4 + q
                if q == 0:
                    pe.wait_ge(stage_ready, c + 1)
                if not isinstance(s, int) or s >= 1:
                    pe.wait_ge(bu_read, s)
                r = slice(32 * q, 32 * q + 32)
                mm(side[:, 0], BST[r, 0], US[r], start=True, stop=True)
                mm(side[:, 1], BST[r, 1], US[r], start=True, stop=True).then_inc(bu_done, 1)

            def cs(c, q):
                s = c * 4 + q
                if q == 0:
                    pe.wait_ge(c_landed, c * 16 + 16)
                    if not isinstance(c, int) or c >= 1:
                        pe.wait_ge(y_read, c)
                pe.wait_ge(state_ready, s + 1)
                r = slice(32 * q, 32 * q + 32)
                mm(side[r, 2], CST[:, q, 0], SB[:, q % 2, 0], start=True, stop=False)
                mm(side[r, 2], CST[:, q, 1], SB[:, q % 2, 1], start=False, stop=True).then_inc(c_done, 1)

            def gates(c, first):
                for j in range(8):
                    if j % 4 == 0:
                        take_bank(c * 2 + (B_GATE + j // 4))
                    product(c * 8 + (U_GATE + j), j % 4, 1 - j // 4, HH, HL, 4 * (j % 4), j % 4 == 0, j % 4 == 3)
                    if j % 2 == 0:
                        bu(c, j // 2)
                        if j >= 4:
                            cs(c, j // 2 - 2)
                        elif not first:
                            cs(c - 1, j // 2 + 2)

            gates(0, True)
            with pe.Fori(1, CT) as c:
                gates(c, False)
            cs(CT - 1, 2)
            cs(CT - 1, 3)

            def glu(i, first):
                for j in range(4):
                    if j % 2 == 0:
                        take_bank(i * 2 + (B_GLU + j // 2))
                    if first and j < 2:
                        pe.wait_ge(yl_ready, 4 * j + 4)
                    product(i * 4 + (U_GLU + j), j, 1 - j // 2, YH, YL, 4 * (j % 2), j % 2 == 0, j % 2 == 1)

            glu(0, True)
            with pe.Fori(1, 4) as i:
                glu(i, False)

            def branches(p, first):
                for j in range(4):
                    if j % 2 == 0:
                        take_bank(p * 2 + (B_BR + j // 2))
                    if first and j < 2:
                        pe.wait_ge(oal_ready, 4 * j + 4)
                    if first and j >= 2:
                        pe.wait_ge(osl_ready, 4 * (j - 1))
                    xh, xl = (OAH, OAL) if j < 2 else (OSH, OSL)
                    product(p * 4 + (U_BR + j), j, 1 - j // 2, xh, xl, 4 * (j % 2), j % 2 == 0, j % 2 == 1)

            branches(0, True)
            with pe.Fori(1, 8) as p:
                branches(p, False)

            def project(i, first):
                for j in range(8):
                    if j % 4 == 0:
                        take_bank(i * 2 + (B_OUT + j // 4))
                    if first and j < 4:
                        pe.wait_ge(ml_ready, 2 * j + 2)
                    product(i * 8 + (U_OUT + j), j % 4, 1 - j // 4, MH, ML, 4 * (j % 4), j % 4 == 0, j % 4 == 3)

            project(0, True)
            with pe.Fori(1, 4) as i:
                project(i, False)
            pe.wait_ge(sum_ready, 1)
            mm(side[:, 3], ONES[:], SQS[:, 0], start=True, stop=True).then_inc(stat_done, 1)

            def up(n0, b0, first):
                for j in range(8):
                    if j % 4 == 0:
                        take_bank(b0 + j // 4)
                    if first and j < 4:
                        pe.wait_ge(h2l_ready, 2 * j + 2)
                    product(n0 + j, j % 4, 1 - j // 4, MH, ML, 4 * (j % 4), j % 4 == 0, j % 4 == 3)
                    if first and j < 4:
                        for k in (2 * j, 2 * j + 1):
                            pe.wait_ge(h2sq_ready, k + 1)
                            for t in range(2):
                                ins = mm(side[:, 2], ONES[:], SQ[:, k % 2, t], start=k + t == 0,
                                         stop=k == 7 and t == 1)
                            ins.then_inc(stat_done if k == 7 else h2sq_used, 1)

            def down(n0, b0, buf, halves):
                for m in range(8):
                    take_bank(b0 + m)
                    if m == 0:
                        pe.wait_ge(al_ready, halves)
                    product(n0 + m, m % 4, 1 - m % 2, AH[:, buf], AL[:, buf], 0, True, True)

            up(U_UP, B_UP, True)
            up(U_MLP, B_MLP, False)
            down(U_MLP + 8, B_MLP + 2, 0, 2)
            with pe.Fori(0, (N_GROUP - 2) // 2) as i:
                for h in range(2):
                    n0, b0 = i * 32 + (U_MLP + 16 + 16 * h), i * 20 + (B_MLP + 10 + 10 * h)
                    up(n0, b0, False)
                    down(n0 + 8, b0 + 2, 1 - h, i * 4 + (4 + 2 * h))
            down(U_TAIL, B_TAIL, 1, 2 * N_GROUP)
            pe.wait_ge(sum_ready, 2)
            mm(side[:, 3], ONES[:], SQS[:, 0], start=True, stop=True).then_inc(stat_done, 1)


def units(w, blocks, kts):
    t = w.reshape(w.shape[0] // P, P, w.shape[1] // P, P)
    got = [t[k:k + 4][:, :, list(b)].transpose(1, 0, 2, 3).reshape(P, 1024)
           for b in blocks for k in range(kts[0], kts[1], 4)]
    return got


def in_pairs(n):
    return [(2 * b, 2 * b + 1) for b in range(n)]


def head_order():
    return np.concatenate([np.arange(h * HEAD, h * HEAD + HEAD) for i in range(8) for h in (i, 8 + i)])


def stream(w_in, w_glu, w_branch, w_out, w_up, w_down):
    q = N_Q * HEAD
    kv = 2 * N_KV * HEAD
    order = head_order()
    g = []
    g += units(w_in[:, :q][:, order], in_pairs(4), (0, KT))
    g += units(w_in[:, q:q + kv], in_pairs(1), (0, KT))
    g += units(w_in[:, q + kv:q + kv + SSM_W], in_pairs(4), (0, KT))
    g += units(w_in[:, q + kv + SSM_W:], in_pairs(16), (0, KT))
    g += units(w_glu, [(b, 8 + b) for b in range(8)], (0, 8))
    attn, ssm = w_branch[:q][order], w_branch[q:]
    for p in range(8):
        g += units(attn, [(2 * p, 2 * p + 1)], (0, 8)) + units(ssm, [(2 * p, 2 * p + 1)], (0, 8))
    g += units(w_out, in_pairs(8), (0, KT))
    up = [units(w_up, [(4 * h, 4 * h + 1), (4 * h + 2, 4 * h + 3)], (0, KT)) for h in range(N_GROUP)]
    down = [units(w_down, in_pairs(8), (4 * h, 4 * h + 4)) for h in range(N_GROUP)]
    g += up[0]
    for h in range(1, N_GROUP):
        g += up[h] + down[h - 1]
    g += down[-1]
    assert len(g) == N_UNIT
    return np.stack(g)


def by_partition(v):
    return v.reshape(-1, P).T


def shape_constants():
    half = ROT // 2
    inv = np.float32(THETA) ** (-np.arange(half, dtype=np.float32) * np.float32(2.0) / np.float32(ROT))
    ang = np.arange(T, dtype=np.float32)[None, :] * inv[:, None].astype(np.float32)
    cos, sin = np.ones((P, T), np.float32), np.zeros((P, T), np.float32)
    perm = np.zeros((P, P), np.float32)
    for h in (0, HEAD):
        for d in range(half):
            for e in (d, d + half):
                cos[h + e], sin[h + e] = np.cos(ang[d]), np.sin(ang[d])
            perm[h + d + half, h + d] = -1.0
            perm[h + d, h + d + half] = 1.0
    far = np.finfo(np.float32).max
    query, key = np.arange(P)[:, None], np.arange(2 * P)[None, :]
    rel = query + P - key
    inside = (rel >= 0) & (rel < P)
    first = np.where(inside & (key >= P), far, -far).astype(np.float32)
    rest = np.where(inside, far, -far).astype(np.float32)
    return np.concatenate([cos, sin, perm, np.eye(P, dtype=np.float32), first, rest], axis=1)


def parameter_rows(x):
    by_channel = np.repeat(x.reshape(CT, 8, SSM_S).transpose(1, 0, 2)[:, None], SSM_C, axis=1).reshape(P, NW)
    by_state = x.reshape(ST, P).T
    return np.concatenate([by_channel, by_state], axis=1)


def padded_b(b):
    out = np.zeros((4, 2, SSM_C, CT, 2, SSM_S), np.float32)
    x = b.reshape(CT, 4, 2, SSM_S, SSM_C)
    for g in range(2):
        out[:, g, :, :, g] = x[:, :, g].transpose(1, 3, 0, 2)
    return out.reshape(P, CT * P)


def padded_c(re, im):
    out = np.zeros((CT, 2, SSM_S, 4, 2, 2, SSM_C), np.float32)
    for r, c in enumerate((re, im)):
        x = c.reshape(CT, 4, 2, SSM_C, SSM_S)
        for g in range(2):
            out[:, g, :, :, r, g] = x[:, :, g].transpose(0, 3, 1, 2)
    return out.reshape(CT, P, 256)


def kernel(**inputs):
    import concourse.bacc as bacc
    from concourse.bass_utils import run_bass_kernel_spmd

    a = {k: np.asarray(v) for k, v in inputs.items()}
    one = {k: v[0] for k, v in a.items() if k != "x"}
    heads = [h for i in range(8) for h in (i, 8 + i)]
    cols = np.zeros((P, 32), np.float32)
    cols[:, 0:8] = by_partition(one["d_skip"].reshape(-1))
    cols[:, 8:24] = one["sinks"][heads][None, :]
    cols[:, 24] = EPS
    arrays = {
        "wstream": stream(one["w_in"], one["w_glu"], one["w_branch"], one["w_out"], one["w_up"], one["w_down"]),
        "x_t": np.ascontiguousarray(a["x"][0].T).reshape(KT, P, T),
        "gains": np.concatenate([by_partition(one[k]) for k in
                                 ("norm_mix_pre", "norm_mix_post", "norm_mlp_pre", "norm_mlp_post")], axis=1),
        "params": np.stack([parameter_rows(one["lam_re"]), parameter_rows(one["lam_im"]),
                            parameter_rows(np.repeat(one["log_dt"][:, None], SSM_S, axis=1))]),
        "b_pad": np.stack([padded_b(one["b_re"]), padded_b(one["b_im"])]),
        "c_pad": padded_c(one["c_re"], one["c_im"]),
        "consts": shape_constants(),
        "cols": cols,
    }
    arrays = {k: np.ascontiguousarray(v) for k, v in arrays.items()}
    nc = bacc.Bacc("TRN2", target_bir_lowering=False, num_devices=1)
    args = [nc.dram_tensor(k, v.shape, mybir.dt.from_np(v.dtype), kind="ExternalInput").ap()
            for k, v in arrays.items()]
    out = nc.dram_tensor("out_t", (KT // 2, P, 2 * T), F32, kind="ExternalOutput").ap()
    build(nc, *args, out)
    got = run_bass_kernel_spmd(nc, [arrays], core_ids=[0]).results[0]["out_t"]
    y = got.reshape(KT // 2, P, 2, T).transpose(0, 2, 1, 3).reshape(D, T)
    return np.ascontiguousarray(y.T)[None]
```

```python
from contextlib import ExitStack

import numpy as np

import concourse.bass as bass
from concourse import mybir

F32 = mybir.dt.float32
F32R = mybir.dt.float32r
I32 = mybir.dt.int32
ALU = mybir.AluOpType
ACT = mybir.ActivationFunctionType
AX = mybir.AxisListType.X

P = 128
T = 512
D = 2048
FF = 4 * D
HEAD = 64
N_Q, N_KV = 16, 2
SSM_W, SSM_G, SSM_C, SSM_S = 1024, 64, 16, 64
ROT, THETA = 16, 500000.0
EPS = 1e-6
KT = D // P
CT = SSM_W // P
ST = SSM_G * SSM_S // P
NW = SSM_S * CT
NP = NW + ST
RING = 4
EJ = 16
NPOW = 9

U_Q, U_U, U_GATE = 0, 20, 36
U_GLU, U_BR, U_OUT, U_UP = 100, 116, 148, 180
U_MLP = U_UP + 8
N_GROUP = FF // 512
U_TAIL = U_MLP + 16 * (N_GROUP - 1)
N_UNIT = U_TAIL + 8
B_GATE, B_GLU, B_BR, B_OUT, B_UP = 9, 25, 33, 49, 57
B_MLP = B_UP + 2
B_TAIL = B_MLP + 10 * (N_GROUP - 1)
N_SLOT0 = 24

LOG2E = 1.4426950408889634
LN2_HI, LN2_LO = 0.693359375, -2.12194440e-4
MAGIC = 12582912.0
EXP_COEF = [1 / 5040., 1 / 720., 1 / 120., 1 / 24., 1 / 6., 0.5, 1.0]
TWO_PI = (6.28125, 0.00193500518798828125, 3.0199159819e-7)
PI_SAFE = 3.1415925


class Count:

    def __init__(self, sem):
        self.sem, self.n, self.turn, self.per = sem, 0, None, 0

    def value(self):
        return self.n if self.turn is None else self.turn * self.per + self.n

    def enter(self, turn, first, per):
        self.turn, self.per, self.at = turn, per, self.n
        self.n -= first * per

    def leave(self, first, end):
        done = self.n + first * self.per - self.at
        assert done == self.per, f"{self.sem}: {done} a turn, {self.per} given"
        self.n = self.at + (end - first) * self.per
        self.turn, self.per = None, 0


def build(nc, wstream, xT, gains, params, b_pad, c_pad, consts, cols, out):
    gate_dram = nc.dram_tensor("gate_scratch", [16, P, 2 * T], F32, kind="Internal").ap()
    x1_dram = nc.dram_tensor("x1_scratch", [8, P, 2 * T], F32, kind="Internal").ap()
    b_dram = nc.dram_tensor("b_scratch", [ST, 3, 32, 2 * P], F32, kind="Internal").ap()
    base = (nc.sbuf_base + 31) // 32 * 32

    def at(name, shape, kib, dt=F32):
        return nc.alloc_sbuf_tensor_at(name, [P] + shape, dt, offset=base + int(kib * 1024))

    RAW = at("w_raw", [RING, 4, 256], 0)
    WH = at("w_hi", [RING, 4, 256], 16, F32R)
    WL = at("w_lo", [RING, 4, 256], 32, F32R)
    HH = at("h_hi", [KT, T], 48, F32R)
    HL = at("h_lo", [KT, T], 80, F32R)
    YH = at("y_hi", [CT, T], 48, F32R)
    YL = at("y_lo", [CT, T], 64, F32R)
    OSH = at("o_ssm_hi", [CT, T], 80, F32R)
    OSL = at("o_ssm_lo", [CT, T], 96, F32R)
    ML = at("m_lo", [KT, T], 48, F32R)
    Z = at("mixed", [KT, T], 80)
    ACC = at("mlp_acc", [KT, T], 80)
    XT = at("x", [KT, T], 112)
    U = at("u", [CT, T], 112)
    Q = at("q", [8, T], 128)
    MH = at("m_hi", [KT, T], 112, F32R)
    X1F = at("x1_all", [KT, T], 112)
    NPB = 12
    PB = at("probs", [NPB, 2, 256], 144)
    PTB = at("probs_t", [4, T], 168)
    ROPE = at("rope", [2, T], 168)
    KV = at("kv_raw", [2, T], 172)
    SQX = at("x_squares", [2, 4, T], 151)
    KTOK = at("k_t", [P + T], 176)
    VTOK = at("v_tok", [5, P], 178.5)
    MASK = at("mask", [2, 256], 181)
    SUM0 = at("square_sum", [4, T], 183)
    E0 = at("rotation_start", [ST, 2, EJ], 187)
    BB = at("b_bar", [CT, 2, P], 191)
    tmp = [at(f"param{k}", [NP], 144 + 2.125 * k) for k in range(11)]
    BHL = [at(f"b_bar_{x}", [CT, 2, P], kib, F32R) for x, kib in (("hi", 144), ("lo", 152))]
    BT = [at(f"b_bar_tmp{k}", [CT, P], 152 + 4 * k) for k in range(2)]
    ROT_T = at("rotation", [2, 2, T], 144)
    ROT_C = at("rotation_by_cos", [2, T // 2], 152)
    ROT_S = at("rotation_by_sin", [2, T // 2], 184.5)
    M1 = at("prod_cos", [2, T], 154)
    M2 = at("prod_sin", [2, T], 158)
    WI = at("scan_in", [2, T], 162)
    SB = at("states", [2, 2, T], 166)
    GS = at("gate_stage", [2, 2, T], 174)
    BW = at("b_weights", [2, P], 182, F32R)
    US = at("u_rows", [T], 195, F32R)
    BWD, USD = at("b_weights_landed", [2, P], 183), at("u_rows_landed", [T], 197)
    UHL = at("u_hi_lo", [2, T], 191, F32R)
    PWT = at("powers_tile", [NPOW - 4, 2], 184)
    OAH = at("o_attn_hi", [CT, T], 144, F32R)
    OAL = at("o_attn_lo", [CT, T], 160, F32R)
    SG = at("glu_gate", [T], 176)
    OT = at("glu_out", [T], 178)
    GA = at("gate_attn", [2, T], 180)
    GB = at("gate_ssm", [2, T], 184)
    TA = at("branch_attn", [2, T], 188)
    TB = at("branch_sum", [2, T], 192)
    SQ = at("squares", [2, 2, T], 176)
    H2 = at("mlp_input", [2, 2, T], 176)
    SQS = at("square_sums", [2, T], 184)
    X1 = at("x1", [KT, T], 144)
    AH = at("a_hi", [2, 4, T], 144, F32R)
    AL = at("a_lo", [2, 4, T], 160, F32R)
    TT = at("up_normed", [2, T], 188)
    AA = at("a", [2, T], 192)
    RSTD = at("rstd", [T], 199)
    IDENT = at("ident", [P], 201)
    PERM = at("perm", [P], 201.5)
    ONES = at("ones", [P], 202)
    CST = at("c_stage", [4, 2, 32], 203.5)
    PW = at("powers", [NPOW, 2, ST], 204.5)
    MAG = at("decay", [ST], 206.75)
    GAIN = at("gain", [4, KT], 206.875)
    COLS = at("cols", [32], 207.125)
    NMX = at("softmax_neg_max", [2, 8], 207.25)
    SES = at("softmax_exp_sink", [2, 8], 207.3125)
    MX = at("softmax_max", [2, 8], 207.375)
    SMK = at("softmax_sink", [2, 8], 207.4375)
    RS = at("softmax_sum", [2, 8], 207.5)
    assert 207.5625 * 1024 + base <= nc.sbuf_usable_end
    D_SKIP, SINK, EPS_C = 0, 8, 24

    with ExitStack() as ctx:
        main = ctx.enter_context(nc.psum_tensor("main", [P, 4, T], F32))
        side = ctx.enter_context(nc.psum_tensor("side", [P, 4, T], F32))

        def sem(name):
            return ctx.enter_context(nc.semaphore(name))

        raw_landed = [sem(f"raw_landed{s}") for s in range(RING)]
        hi_ready, lo_ready, unit_done = sem("hi_ready"), sem("lo_ready"), sem("unit_done")
        bank_read = sem("bank_read")
        x_landed = [sem(f"x_landed{s}") for s in range(4)]
        consts_landed, small_landed, par_landed, b_landed = (
            sem("consts_landed"), sem("small_landed"), sem("par_landed"), sem("b_landed"))
        ones_set, pads_set = sem("ones_set"), sem("pads_set")
        xh_ready, xsq_ready, xl_ready, xsum_step = (
            sem("xh_ready"), sem("xsq_ready"), sem("xl_ready"), sem("xsum_step"))
        stat_done, std_ready = sem("stat_done"), sem("std_ready")
        rope_mm, rope_free, vt_done, v_ready = (
            sem("rope_mm"), sem("rope_free"), sem("vt_done"), sem("v_ready"))
        angle_ready, trig_ready, bb_ready = sem("angle_ready"), sem("trig_ready"), sem("bb_ready")
        scores_done, scores_read, exp_ready, nmax_ready, probs_ready = (
            sem("scores_done"), sem("scores_read"), sem("exp_ready"), sem("nmax_ready"), sem("probs_ready"))
        trans_done, pt_ready, pv_done, o_ready = (
            sem("trans_done"), sem("pt_ready"), sem("pv_done"), sem("o_ready"))
        bh_ready, bl_ready, b_stored = sem("bh_ready"), sem("bl_ready"), sem("b_stored")
        uh_ready, ul_ready, rows_landed, rows_ready = (
            sem("uh_ready"), sem("ul_ready"), sem("rows_landed"), sem("rows_ready"))
        bu_done, bu_read, state_ready, c_done, y_read, y_ready = (
            sem("bu_done"), sem("bu_read"), sem("state_ready"),
            sem("c_done"), sem("y_read"), sem("y_ready"))
        c_landed, gate_ready, gate_stored = (
            [sem("c_landed0"), sem("c_landed1")], sem("gate_ready"), [sem("gate_stored0"), sem("gate_stored1")])
        rot_ready, rot_step, start_ready = sem("rot_ready"), sem("rot_step"), sem("start_ready")
        yh_ready, yl_ready, oah_ready, oal_ready = (
            sem("yh_ready"), sem("yl_ready"), sem("oah_ready"), sem("oal_ready"))
        sig_ready, osh_ready, osl_ready = sem("sig_ready"), sem("osh_ready"), sem("osl_ready")
        ga_landed, gb_landed, br_ready, mh_ready, ml_ready = (
            sem("ga_landed"), sem("gb_landed"), sem("br_ready"), sem("mh_ready"), sem("ml_ready"))
        sq_ready, sq_used, sum_ready = sem("sq_ready"), sem("sq_used"), sem("sum_ready")
        xr_landed, x1_ready, x1_stored, h2h_ready, h2l_ready = (
            sem("xr_landed"), sem("x1_ready"), sem("x1_stored"), sem("h2h_ready"), sem("h2l_ready"))
        h2sq_ready, h2sq_used = sem("h2sq_ready"), sem("h2sq_used")
        a_ready, ah_ready, al_ready = sem("a_ready"), sem("ah_ready"), sem("al_ready")
        last_tile, last_sq = sem("last_tile"), sem("last_sq")
        fsq_ready, fsq_used, x1_back, product_ready, out_stored = (
            sem("fsq_ready"), sem("fsq_used"), sem("x1_back"), sem("product_ready"), sem("out_stored"))
        out_ready = {"DVE": sem("out_ready_dve"), "Pool": sem("out_ready_pool")}
        dve_step = sem("dve_step")

        ADDER = ["Pool", "Pool", "DVE", "Pool", "Pool", "DVE", "Pool", "DVE"]

        block = ctx.enter_context(nc.Block())

        def group_of(slot, first):
            return [slot - first] if 0 <= slot - first < 8 else []

        @block.sync
        def _(sp):
            for n in range(RING):
                if n >= 1:
                    sp.wait_ge(x_landed[(2 * n - 1) % 4], 16 * ((2 * n - 1) // 4 + 1))
                sp.dma_start(RAW[:, n], wstream[n].rearrange("p (k m) -> p k m", k=4)).then_inc(raw_landed[n], 16)
            with sp.Fori(1, N_UNIT // RING) as i:
                for s in range(RING):
                    sp.wait_ge(lo_ready, (i - 1) * RING + s + 1)
                    sp.dma_start(RAW[:, s], wstream[i * RING + s].rearrange("p (k m) -> p k m", k=4)
                                 ).then_inc(raw_landed[s], 16)
            for k in range(KT // 2):
                sp.wait_ge(out_ready[ADDER[k]], ADDER[:k + 1].count(ADDER[k]))
                sp.dma_start(out[k].rearrange("p (a t) -> p a t", a=2), ACC[:, 2 * k:2 * k + 2]).then_inc(out_stored, 16)
            sp.wait_ge(out_stored, 16 * (KT // 2))

        @block.gpsimd
        def _(pool):
            nc.gpsimd.memset(ONES[:], 1.0).then_inc(ones_set, 1)
            for r in range(KT // 2):
                if r >= 3:
                    pool.wait_ge(x_landed[(r - 3) % 4], 16 * ((r - 3) // 4 + 1))
                pool.dma_start(XT[:, 2 * r:2 * r + 2], xT[2 * r:2 * r + 2].rearrange("k p t -> p k t")
                               ).then_inc(x_landed[r % 4], 16)
            nc.gpsimd.memset(KTOK[:, 0:P], 0.0)
            nc.gpsimd.memset(VTOK[:, 0], 0.0).then_inc(pads_set, 1)
            for k in range(3):
                pool.dma_start(tmp[k][:], params[k]).then_inc(par_landed, 16)
            pool.dma_start(ROPE[:], consts[:, 0:2 * T].rearrange("p (a t) -> p a t", a=2)).then_inc(consts_landed, 16)
            pool.dma_start(PERM[:], consts[:, 1024:1152]).then_inc(consts_landed, 16)
            pool.dma_start(IDENT[:], consts[:, 1152:1280]).then_inc(consts_landed, 16)
            pool.dma_start(MASK[:], consts[:, 1280:1792].rearrange("p (a t) -> p a t", a=2)).then_inc(consts_landed, 16)
            for r in range(2):
                pool.dma_start(BB[:, :, r], b_pad[r].rearrange("p (c s) -> p c s", c=CT)).then_inc(b_landed, 16)
            pool.wait_ge(bl_ready, 1)
            for q in range(4):
                for row, part in enumerate((0, 0, 1)):
                    pool.dma_start(b_dram[q:ST:4, row].rearrange("c r m -> r c m"),
                                   BHL[part][32 * q:32 * q + 32].rearrange("r c x m -> r c (x m)").bitcast(F32)
                                   ).then_inc(b_stored, 16)

            rstep = Count(rot_step)

            def rlink(ins):
                ins.then_inc(rot_step, 1)
                rstep.n += 1
                pool.wait_ge(rot_step, rstep.value())

            def rotation(c, q):
                s = c * 4 + q
                if not isinstance(s, int) or s >= 2:
                    pool.wait_ge(state_ready, s - 1)
                rot = ROT_T[:, q % 2]
                nc.gpsimd.tensor_copy(PWT[:], PW[:, 4:NPOW, :, s])
                rlink(nc.gpsimd.tensor_copy(rot[:, :, 0:EJ], E0[:, s]))
                n = EJ
                while n < T:
                    k = n.bit_length() - 5
                    pr, pi = (PWT[:, k, x:x + 1].unsqueeze(2).to_broadcast([P, 2, n]) for x in range(2))
                    tc, ts_ = ROT_C[:, :, 0:n], ROT_S[:, :, 0:n]
                    nc.gpsimd.tensor_tensor(tc, rot[:, :, 0:n], pr, ALU.mult)
                    rlink(nc.gpsimd.tensor_tensor(ts_, rot[:, :, 0:n], pi, ALU.mult))
                    nc.gpsimd.tensor_tensor(rot[:, 0, n:2 * n], tc[:, 0], ts_[:, 1], ALU.subtract)
                    ins = nc.gpsimd.tensor_tensor(rot[:, 1, n:2 * n], tc[:, 1], ts_[:, 0], ALU.add)
                    n *= 2
                    if n < T:
                        rlink(ins)
                    else:
                        ins.then_inc(rot_ready, 1)
                        pool.wait_ge(rot_ready, s + 1)

            def load_c(c, half):
                count = c * 4 - 2 + 2 * half
                if not isinstance(c, int) or c >= 1:
                    pool.wait_ge(c_done, count)
                pool.dma_start(CST[:, 2 * half:2 * half + 2], c_pad[c][:, 128 * half:128 * half + 128]
                               .rearrange("p (q r m) -> p q r m", q=2, r=2)).then_inc(c_landed[half], 16)

            def rotations(c):
                rotation(c, 0)
                load_c(c, 0)
                rotation(c, 1)
                rotation(c, 2)
                load_c(c, 1)
                rotation(c, 3)

            pool.wait_ge(start_ready, 1)
            pool.wait_ge(o_ready, 8)
            rotations(0)
            with pool.Fori(1, CT) as c:
                rstep.enter(c, 1, 4 * 10)
                rotations(c)
                rstep.leave(1, CT)
            for r in range(2):
                pool.wait_ge(gate_stored[r], 16 * CT)
            pool.wait_ge(y_read, CT)

            def load_gates(p):
                pool.dma_start(GA[:], gate_dram[p].rearrange("p (a t) -> p a t", a=2)).then_inc(ga_landed, 16)
                pool.dma_start(GB[:], gate_dram[p + 8].rearrange("p (a t) -> p a t", a=2)).then_inc(gb_landed, 16)

            load_gates(0)
            with pool.Fori(1, 8) as p:
                pool.wait_ge(bank_read, p * 2 + B_BR)
                load_gates(p)
            pool.wait_ge(unit_done, U_OUT)
            for k in range(KT // 4):
                pool.dma_start(X1[:, 4 * k:4 * k + 4], xT[4 * k:4 * k + 4].rearrange("k p t -> p k t")
                               ).then_inc(xr_landed, 16)
            for k in range(KT // 2):
                pool.wait_ge(h2h_ready, k + 1)
                t = slice(2 * k, 2 * k + 2)
                nc.gpsimd.tensor_tensor(ML[:, t], H2[:, k % 2], MH[:, t].bitcast(F32), ALU.subtract
                                        ).then_inc(h2l_ready, 1)
            pool.wait_ge(x1_stored, 16 * KT // 2)
            pool.wait_ge(unit_done, U_TAIL - 8)
            for k in range(KT // 4):
                pool.dma_start(X1F[:, 4 * k:4 * k + 4], x1_dram[2 * k:2 * k + 2].rearrange("k p (a t) -> p k a t", a=2)
                               ).then_inc(x1_back, 16)
            pool.wait_ge(x1_back, 16 * KT // 4)
            for k in range(KT // 2):
                if ADDER[k] == "Pool":
                    pool.wait_ge(product_ready, k + 1)
                    o = ACC[:, 2 * k:2 * k + 2]
                    nc.gpsimd.tensor_tensor(o, o, X1F[:, 2 * k:2 * k + 2], ALU.add).then_inc(out_ready["Pool"], 1)

        @block.scalar
        def _(act):
            def hi(n, s, turns):
                act.wait_ge(raw_landed[s], turns * 16 + 16)
                if not isinstance(n, int) or n >= RING:
                    act.wait_ge(unit_done, n - (RING - 1))
                nc.scalar.activation(WH[:, s], RAW[:, s], ACT.Copy).then_inc(hi_ready, 1)

            def unit(n0, j, i=0, per=0):
                hi(i * per + (n0 + j), (n0 + j) % RING, i * (per // RING) + (n0 + j) // RING)

            act.dma_start(GAIN[:], gains.rearrange("p (a k) -> p a k", a=4)).then_inc(small_landed, 16)
            act.dma_start(COLS[:], cols).then_inc(small_landed, 16)
            unit(0, 0)
            act.wait_ge(small_landed, 32)
            for k in range(KT):
                if k % 2 == 0:
                    act.wait_ge(x_landed[k // 2 % 4], 16 * (k // 8 + 1))
                nc.scalar.activation(HH[:, k], XT[:, k], ACT.Copy, scale=GAIN[:, 0, k:k + 1]).then_inc(xh_ready, 1)
                if k % 4 == 3:
                    if k < KT - 1:
                        unit(k // 4 + 1, 0)
            for n in range(4):
                if n >= 2:
                    act.wait_ge(xsum_step, n - 1)
                nc.scalar.activation(SQX[:, n % 2], XT[:, 4 * n:4 * n + 4], ACT.Square).then_inc(xsq_ready, 1)
                if n == 1:
                    unit(4, 0)
            unit(5, 0)

            def attention(slot):
                for k in range(4):
                    for g in group_of(slot, N_SLOT0 + 2):
                        a = 4 * g + k
                        act.wait_ge(trans_done, a + 1)
                        if a >= 4:
                            act.wait_ge(pv_done, a - 3)
                        nc.scalar.activation(PTB[:, a % 4], side[:, 2], ACT.Copy).then_inc(pt_ready, 1)
                    for g in group_of(slot, N_SLOT0 + 1):
                        if k == 0:
                            act.wait_ge(nmax_ready, g + 1)
                        for h in range(4 * k, 4 * k + 4) if k < 2 else ():
                            p = PB[:, (4 * g + h // 2) % NPB, h % 2]
                            nc.scalar.activation(p, p, ACT.Exp, bias=NMX[:, g % 2, h:h + 1],
                                                 accum_out=RS[:, g % 2, h:h + 1])
                        if k == 1:
                            nc.scalar.activation(SES[:, g % 2], SMK[:, g % 2], ACT.Exp).then_inc(exp_ready, 1)
                for g in group_of(slot, N_SLOT0 + 3):
                    act.wait_ge(pv_done, 4 * g + 4)
                    n, i = g // 2, 4 * (g % 2)
                    nc.scalar.activation(Q[:, i:i + 4, n * P:n * P + P],
                                         side[:, 3].rearrange("p (i t) -> p i t", i=4), ACT.Copy).then_inc(o_ready, 1)

            for n in range(6, U_GATE):
                unit(n, 0)
                if n == 6:
                    act.wait_ge(stat_done, 1)
                    nc.scalar.activation(RSTD[:], side[:, 3], ACT.Sqrt, bias=COLS[:, EPS_C:EPS_C + 1],
                                         scale=1.0 / D).then_inc(std_ready, 1)
                if n == 19:
                    act.wait_ge(bb_ready, 1)
                    nc.scalar.activation(BHL[0][:], BB[:], ACT.Copy).then_inc(bh_ready, 1)
                if n == 12:
                    act.wait_ge(angle_ready, 1)
                    nc.scalar.activation(tmp[6][:], tmp[4][:], ACT.Sin)
                    nc.scalar.activation(tmp[7][:], tmp[5][:], ACT.Sin).then_inc(trig_ready, 1)
                if n == 23:
                    act.wait_ge(vt_done, 1)
                    act.wait_ge(pads_set, 1)
                    nc.scalar.activation(VTOK[:, 1:5], side[:, 2].rearrange("p (n d) -> p n d", n=4),
                                         ACT.Copy).then_inc(v_ready, 1)
                if n >= N_SLOT0 + 2:
                    attention(n - 2)

            def u_hi(c):
                if not isinstance(c, int) or c >= 1:
                    act.wait_ge(rows_landed, c * 256)
                nc.scalar.activation(UHL[:, 0], U[:, c], ACT.Copy).then_inc(uh_ready, 1)

            def move(c, q):
                s, r = c * 4 + q, slice(32 * q, 32 * q + 32)
                if q == 0:
                    act.wait_ge(ul_ready, c + 1)
                if not isinstance(s, int) or s >= 1:
                    act.wait_ge(rows_ready, s)
                act.dma_start(BWD[0:96], b_dram[s].rearrange("h r (x m) -> (h r) x m", x=2)).then_inc(rows_landed, 16)
                for row, part in enumerate((0, 1, 0)):
                    act.dma_start(USD[32 * row:32 * row + 32], UHL[r, part].bitcast(F32)).then_inc(rows_landed, 16)

            def stage(c, q):
                s = c * 4 + q
                act.wait_ge(rows_landed, s * 64 + 64)
                if not isinstance(s, int) or s >= 1:
                    act.wait_ge(bu_done, s)
                nc.scalar.activation(BW[0:96], BWD[0:96], ACT.Copy)
                nc.scalar.activation(US[0:96], USD[0:96], ACT.Copy).then_inc(rows_ready, 1)

            def sigmoid(count, buf):
                act.wait_ge(bank_read, count + B_GATE)
                nc.scalar.activation(GS[:, buf], GS[:, buf], ACT.Sigmoid).then_inc(gate_ready, 1)

            def store_gate(count, buf, after_other=False):
                act.wait_ge(gate_ready, count)
                if after_other:
                    act.wait_ge(gate_stored[1], (count - 1) * 8)
                act.dma_start(gate_dram[count - 1].rearrange("p (a t) -> p a t", a=2), GS[:, buf]
                              ).then_inc(gate_stored[buf], 16)

            def gelu(c, count):
                act.wait_ge(y_read, count)
                nc.scalar.activation(U[:, c], U[:, c], ACT.Gelu_apprx_tanh).then_inc(y_ready, 1)

            for j in range(8):
                unit(U_GATE, j)
                if j == 0:
                    act.wait_ge(bank_read, 6)
                    u_hi(0)
                    attention(U_GATE - 2)
                    act.wait_ge(b_stored, 16 * 12)
                if j % 2 == 0:
                    move(0, j // 2)
                else:
                    stage(0, j // 2)
                if j == 5:
                    sigmoid(1, 0)
                if j == 6:
                    store_gate(1, 0)
            with act.Fori(1, CT) as c:
                for j in range(8):
                    unit(U_GATE, j, c, 8)
                    if j == 0:
                        u_hi(c)
                    if j % 2 == 0:
                        move(c, j // 2)
                    else:
                        stage(c, j // 2)
                    if j == 1:
                        sigmoid(c * 2, 1)
                    if j == 2:
                        store_gate(c * 2, 1)
                    if j == 4:
                        gelu(c - 1, c)
                    if j == 5:
                        sigmoid(c * 2 + 1, 0)
                    if j == 6:
                        store_gate(c * 2 + 1, 0, True)
            unit(U_GLU, 0)
            unit(U_GLU, 1)
            sigmoid(2 * CT, 1)
            store_gate(2 * CT, 1)

            def y_hi(c):
                nc.scalar.activation(YH[:, c], U[:, c], ACT.Copy).then_inc(yh_ready, 1)

            act.wait_ge(unit_done, U_GLU)
            act.wait_ge(y_ready, CT - 1)
            for c in range(CT - 1):
                y_hi(c)
            gelu(CT - 1, CT)
            act.wait_ge(y_ready, CT)
            y_hi(CT - 1)

            def glu(b, part):
                if part == 0:
                    act.wait_ge(unit_done, U_GLU + 2 * b + 2)
                    act.wait_ge(bank_read, B_GLU + b)
                    nc.scalar.activation(SG[:], main[:, 2 * ((B_GLU + b) % 2) + 1], ACT.Sigmoid).then_inc(sig_ready, 1)
                else:
                    act.wait_ge(bank_read, B_GLU + b + 1)
                    nc.scalar.activation(OSH[:, b], OT[:], ACT.Copy).then_inc(osh_ready, 1)

            for j in range(2, 16):
                unit(U_GLU, j)
                if j == 2:
                    for r in range(2):
                        act.wait_ge(gate_stored[r], 16 * CT)
                    for k in range(CT):
                        nc.scalar.activation(OAH[:, k], Q[:, k], ACT.Copy).then_inc(oah_ready, 1)
                if j % 2 == 1:
                    glu((j - 3) // 2, 0)
                    glu((j - 3) // 2, 1)

            def branch(p, count):
                act.wait_ge(br_ready, count)
                nc.scalar.activation(MH[:, bass.ds(p * 2, 2)], TB[:], ACT.Copy).then_inc(mh_ready, 1)

            for j in range(4):
                unit(U_BR, j)
                if j == 1:
                    glu(7, 0)
                    glu(7, 1)
            with act.Fori(1, 8) as p:
                for j in range(4):
                    unit(U_BR, j, p, 4)
                    if j == 1:
                        branch(p - 1, p)

            def squares(count):
                act.wait_ge(bank_read, count)
                act.wait_ge(sq_used, count - B_OUT)
                nc.scalar.activation(SQ[:, 0], Z[:, bass.ds((count - B_OUT - 1) * 2, 2)], ACT.Square).then_inc(sq_ready, 1)

            for j in range(8):
                unit(U_OUT, j)
                if j == 1:
                    branch(7, 8)
                if j == 5:
                    squares(B_OUT + 1)
            with act.Fori(1, 4) as i:
                for j in range(8):
                    unit(U_OUT, j, i, 8)
                    if j == 1:
                        squares(i * 2 + B_OUT)
                    if j == 5:
                        squares(i * 2 + B_OUT + 1)
            unit(U_UP, 0)
            unit(U_UP, 1)

            def last_squares(n, tiles, blocks):
                for t in range(2):
                    if t == 0:
                        act.wait_ge(last_tile, n + 1)
                    else:
                        act.wait_ge(bank_read, blocks)
                    nc.scalar.activation(SQ[:, 1, t], tiles[:, KT - 2 + t], ACT.Square).then_inc(last_sq, 1)

            last_squares(0, Z, B_UP)
            act.wait_ge(stat_done, 2)
            nc.scalar.activation(RSTD[:], side[:, 3], ACT.Sqrt, bias=COLS[:, EPS_C:EPS_C + 1],
                                 scale=1.0 / D).then_inc(std_ready, 1)
            for k in range(KT // 2):
                act.wait_ge(x1_ready, k + 1)
                if k >= 2:
                    act.wait_ge(h2l_ready, k - 1)
                for t in (2 * k, 2 * k + 1):
                    nc.scalar.activation(H2[:, k % 2, t % 2], X1[:, t], ACT.Copy, scale=GAIN[:, 2, t:t + 1])
                    ins = nc.scalar.activation(MH[:, t], X1[:, t], ACT.Copy, scale=GAIN[:, 2, t:t + 1])
                ins.then_inc(h2h_ready, 1)
                act.dma_start(x1_dram[k].rearrange("p (a t) -> p a t", a=2), X1[:, 2 * k:2 * k + 2]
                              ).then_inc(x1_stored, 16)
                if k % 2 == 1 and k // 2 < 2:
                    unit(U_UP, 2 + k // 2)

            def h2_squares(k):
                if k == 0:
                    act.wait_ge(h2l_ready, KT // 2)
                if k >= 2:
                    act.wait_ge(h2sq_used, k)
                nc.scalar.activation(SQ[:, k % 2], X1[:, 2 * k:2 * k + 2], ACT.Square).then_inc(h2sq_ready, 1)

            for j in range(4, 8):
                unit(U_UP, j)
                if j in (4, 5):
                    for k in range(4 * j - 16, 4 * j - 12):
                        h2_squares(k)
            act.wait_ge(stat_done, 3)
            nc.scalar.activation(RSTD[:], side[:, 3], ACT.Sqrt, bias=COLS[:, EPS_C:EPS_C + 1],
                                 scale=1.0 / D).then_inc(std_ready, 1)
            act.wait_ge(a_ready, 1)
            act.wait_ge(x1_stored, 16 * KT // 2)
            nc.scalar.activation(AH[:, 0, 0:2], AA[:], ACT.Copy).then_inc(ah_ready, 1)

            def a_hi(buf, half, count):
                act.wait_ge(a_ready, count)
                nc.scalar.activation(AH[:, buf, 2 * half:2 * half + 2], AA[:], ACT.Copy).then_inc(ah_ready, 1)

            for j in range(16):
                unit(U_MLP, j)
                if j == 1:
                    a_hi(0, 1, 2)
                if j == 5:
                    a_hi(1, 0, 3)
                if j == 9:
                    a_hi(1, 1, 4)
            with act.Fori(0, (N_GROUP - 2) // 2) as i:
                for j in range(32):
                    unit(U_MLP + 16, j, i, 32)
                    if j % 16 == 5:
                        a_hi(j // 16, 0, i * 4 + (5 + 2 * (j // 16)))
                    if j % 16 == 9:
                        a_hi(j // 16, 1, i * 4 + (6 + 2 * (j // 16)))

            def final_squares(m):
                act.wait_ge(bank_read, B_TAIL + m + 1)
                act.wait_ge(fsq_used, m + 1)
                nc.scalar.activation(SQ[:, 0], ACC[:, 2 * m:2 * m + 2], ACT.Square).then_inc(fsq_ready, 1)

            for j in range(8):
                unit(U_TAIL, j)
                if j >= 3:
                    final_squares(j - 3)
            for m in range(5, 7):
                final_squares(m)
            last_squares(1, ACC, B_TAIL + 8)
            act.wait_ge(stat_done, 4)
            nc.scalar.activation(RSTD[:], side[:, 3], ACT.Sqrt, bias=COLS[:, EPS_C:EPS_C + 1],
                                 scale=1.0 / D).then_inc(std_ready, 1)

        @block.vector
        def _(v):
            step = Count(dve_step)

            def link(ins):
                ins.then_inc(dve_step, 1)
                step.n += 1
                v.wait_ge(dve_step, step.value())

            def link_to(ins, sem_, value):
                ins.then_inc(sem_, 1)
                v.wait_ge(sem_, value)

            tt, stt, ts = nc.vector.tensor_tensor, nc.vector.scalar_tensor_tensor, nc.vector.tensor_scalar

            def lo(n, s):
                v.wait_ge(hi_ready, n + 1)
                tt(WL[:, s], RAW[:, s], WH[:, s].bitcast(F32), ALU.subtract).then_inc(lo_ready, 1)

            def unit(n0, j, i=0, per=0):
                lo(i * per + (n0 + j), (n0 + j) % RING)

            def pair(b):
                return main[:, 2 * (b % 2):2 * (b % 2) + 2]

            def both(ap):
                return ap.unsqueeze(1).to_broadcast([P, 2, T])

            link_to(nc.vector.memset(SUM0[:], 0.0), rope_free, 1)
            v.wait_ge(small_landed, 32)
            unit(0, 0)
            for k in range(KT):
                v.wait_ge(xh_ready, k + 1)
                stt(out=HL[:, k], in0=XT[:, k], scalar=GAIN[:, 0, k:k + 1],
                    in1=HH[:, k].bitcast(F32), op0=ALU.mult, op1=ALU.subtract).then_inc(xl_ready, 1)
                if k % 4 == 3 and k < KT - 1:
                    unit(k // 4 + 1, 0)
            for n in range(4):
                v.wait_ge(xsq_ready, n + 1)
                link_to(tt(SUM0[:], SUM0[:], SQX[:, n % 2], ALU.add), xsum_step, n + 1)
                if n == 1:
                    unit(4, 0)
            link(tt(SUM0[:, 0:2], SUM0[:, 0:2], SUM0[:, 2:4], ALU.add))
            link_to(tt(SUM0[:, 0], SUM0[:, 0], SUM0[:, 1], ALU.add), xsum_step, 5)
            unit(5, 0)

            def exp(part, out_, x, k, r, q):
                if part == 1:
                    return exp_end(out_, k, r, q)
                link(ts(out_, x, -87.336, None, ALU.is_ge))
                link(ts(x, x, -87.336, 88.37, ALU.max, ALU.min))
                link(ts(k, x, LOG2E, MAGIC, ALU.mult, ALU.add))
                link(ts(k, k, -MAGIC, None, ALU.add))
                link(stt(out=r, in0=k, scalar=-LN2_HI, in1=x, op0=ALU.mult, op1=ALU.add))
                link(stt(out=r, in0=k, scalar=-LN2_LO, in1=r, op0=ALU.mult, op1=ALU.add))
                link(ts(q, r, EXP_COEF[0], None, ALU.mult))
                for coef in EXP_COEF[1:3]:
                    link(stt(out=q, in0=q, scalar=coef, in1=r, op0=ALU.add, op1=ALU.mult))

            def exp_end(out_, k, r, q):
                for coef in EXP_COEF[3:]:
                    link(stt(out=q, in0=q, scalar=coef, in1=r, op0=ALU.add, op1=ALU.mult))
                link(stt(out=out_, in0=q, scalar=1.0, in1=out_, op0=ALU.add, op1=ALU.mult))
                link(ts(r.bitcast(I32), k, 127.0, 8388608.0, ALU.add, ALU.mult))
                link(tt(out_, out_, r, ALU.mult))

            A = [x[:] for x in tmp]

            def time_step(part):
                v.wait_ge(par_landed, 48)
                exp(part, A[3], A[2], A[8], A[9], A[10])

            def angles():
                link(tt(A[4], A[1], A[3], ALU.mult))
                link(tt(A[2], A[0], A[3], ALU.mult))
                link(ts(A[8], A[4], 1.0 / (2 * np.pi), MAGIC, ALU.mult, ALU.add))
                link(ts(A[8], A[8], -MAGIC, None, ALU.add))
                for part in TWO_PI:
                    link(stt(out=A[4], in0=A[8], scalar=-part, in1=A[4], op0=ALU.mult, op1=ALU.add))
                link(ts(A[4], A[4], -PI_SAFE, PI_SAFE, ALU.max, ALU.min))
                link(stt(out=A[5], in0=A[4], scalar=-1.0, in1=A[4], op0=ALU.mult, op1=ALU.max))
                link_to(ts(A[5], A[5], -1.0, float(np.pi / 2), ALU.mult, ALU.add), angle_ready, 1)

            def decay(part):
                exp(part, A[3], A[2], A[8], A[9], A[10])
                if part == 1:
                    link(nc.vector.tensor_copy(MAG[:], A[3][:, NW:NP]))

            def coefficients(part):
                w = slice(0, NW)
                if part == 1:
                    return coefficients_end(w)
                v.wait_ge(trig_ready, 1)
                link(nc.vector.tensor_copy(PW[:, 0, 0], A[7][:, NW:NP]))
                link(ts(PW[:, 0, 1], A[6][:, NW:NP], -1.0, None, ALU.mult))
                link(tt(A[7][:, w], A[7][:, w], A[3][:, w], ALU.mult))
                link(tt(A[6][:, w], A[6][:, w], A[3][:, w], ALU.mult))
                link(ts(A[7][:, w], A[7][:, w], -1.0, None, ALU.add))
                link(tt(A[8][:, w], A[0][:, w], A[0][:, w], ALU.mult))
                link(tt(A[9][:, w], A[1][:, w], A[1][:, w], ALU.mult))
                link(tt(A[8][:, w], A[8][:, w], A[9][:, w], ALU.add))
                link(nc.vector.reciprocal(A[8][:, w], A[8][:, w]))

            def coefficients_end(w):
                link(tt(A[2][:, w], A[7][:, w], A[0][:, w], ALU.mult))
                link(tt(A[9][:, w], A[6][:, w], A[1][:, w], ALU.mult))
                link(tt(A[2][:, w], A[2][:, w], A[9][:, w], ALU.add))
                link(tt(A[2][:, w], A[2][:, w], A[8][:, w], ALU.mult))
                link(tt(A[10][:, w], A[6][:, w], A[0][:, w], ALU.mult))
                link(tt(A[9][:, w], A[7][:, w], A[1][:, w], ALU.mult))
                link(tt(A[10][:, w], A[10][:, w], A[9][:, w], ALU.subtract))
                link(tt(A[10][:, w], A[10][:, w], A[8][:, w], ALU.mult))

            def b_bar():
                v.wait_ge(b_landed, 32)

                def spread(x):
                    return x[:, 0:NW].rearrange("p (c s) -> p c s", c=CT).unsqueeze(2).to_broadcast([P, CT, 2, SSM_S])

                def halves(x):
                    return x.rearrange("p c (g s) -> p c g s", g=2)

                br, bi = halves(BB[:, :, 0]), halves(BB[:, :, 1])
                t1, t2 = halves(BT[0][:]), halves(BT[1][:])
                cr, ci = spread(A[2]), spread(A[10])
                link(tt(t1, bi, ci, ALU.mult))
                link(tt(t2, br, ci, ALU.mult))
                link(tt(br, br, cr, ALU.mult))
                link(tt(br, br, t1, ALU.subtract))
                link(tt(bi, bi, cr, ALU.mult))
                link_to(tt(bi, bi, t2, ALU.add), bb_ready, 1)

            def powers():
                t1, t2 = A[8][:, 0:ST], A[9][:, 0:ST]
                for k in range(1, NPOW):
                    c_, s_ = PW[:, k - 1, 0], PW[:, k - 1, 1]
                    tt(t1, c_, c_, ALU.mult)
                    link(tt(t2, s_, s_, ALU.mult))
                    tt(PW[:, k, 0], t1, t2, ALU.subtract)
                    link(stt(out=PW[:, k, 1], in0=c_, scalar=2.0, in1=s_, op0=ALU.mult, op1=ALU.mult))

            def rotation_start():
                link(nc.vector.memset(E0[:, :, 0, 0:1], 1.0))
                link(nc.vector.memset(E0[:, :, 1, 0:1], 0.0))
                for k in range(EJ.bit_length() - 1):
                    n = 1 << k
                    t1 = A[8][:, 0:ST * n].rearrange("p (s j) -> p s j", s=ST)
                    t2 = A[9][:, 0:ST * n].rearrange("p (s j) -> p s j", s=ST)
                    er, ei = E0[:, :, 0, 0:n], E0[:, :, 1, 0:n]
                    pr = PW[:, k, 0].unsqueeze(2).to_broadcast([P, ST, n])
                    pi = PW[:, k, 1].unsqueeze(2).to_broadcast([P, ST, n])
                    tt(t1, er, pr, ALU.mult)
                    link(tt(t2, ei, pi, ALU.mult))
                    link(tt(E0[:, :, 0, n:2 * n], t1, t2, ALU.subtract))
                    tt(t1, er, pi, ALU.mult)
                    link(tt(t2, ei, pr, ALU.mult))
                    ins = tt(E0[:, :, 1, n:2 * n], t1, t2, ALU.add)
                    if 2 * n < EJ:
                        link(ins)
                    else:
                        link_to(ins, start_ready, 1)

            def normed(out_, b):
                v.wait_ge(unit_done, UNIT_END[b])
                link_to(tt(out_, pair(b), both(RSTD[:]), ALU.mult), bank_read, b + 1)

            def rope(x, b):
                w = x.shape[1]
                v.wait_ge(rope_mm, b + 1)
                v.wait_ge(consts_landed, 64)
                t = KV[:, 0] if w == 1 else KV[:]
                xx = x[:, 0] if w == 1 else x
                psum = side[:, 0] if w == 1 else side[:, 0:2]
                cos_ = ROPE[:, 0] if w == 1 else both(ROPE[:, 0])
                sin_ = ROPE[:, 1] if w == 1 else both(ROPE[:, 1])
                return xx, t, psum, cos_, sin_

            def rope_q(b):
                xx, t, psum, cos_, sin_ = rope(Q[:, 2 * b:2 * b + 2], b)
                link(tt(t, psum, sin_, ALU.mult))
                link(tt(xx, xx, cos_, ALU.mult))
                link_to(tt(xx, xx, t, ALU.add), rope_free, b + 2)

            def rope_k():
                v.wait_ge(rope_mm, 5)
                v.wait_ge(vt_done, 1)
                v.wait_ge(pads_set, 1)
                link(tt(KV[:, 1], side[:, 0], ROPE[:, 1], ALU.mult))
                link(tt(KV[:, 0], KV[:, 0], ROPE[:, 0], ALU.mult))
                link_to(tt(KTOK[:, P:P + T], KV[:, 0], KV[:, 1], ALU.add), rope_free, 6)

            UNIT_END = {b: 4 * b + 4 for b in range(9)}

            def normalise(g):
                v.wait_ge(exp_ready, g + 1)
                link(tt(RS[:, g % 2], RS[:, g % 2], SES[:, g % 2], ALU.add))
                link(nc.vector.reciprocal(RS[:, g % 2], RS[:, g % 2]))
                for k in range(8):
                    p = PB[:, (4 * g + k // 2) % NPB, k % 2]
                    ins = ts(p, p, RS[:, g % 2, k:k + 1], None, ALU.mult)
                link_to(ins, probs_ready, g + 1)

            def mask_scores(a):
                v.wait_ge(scores_done, a + 1)
                if a >= NPB:
                    v.wait_ge(trans_done, a - NPB + 1)
                mask = MASK[:, 0 if a < 8 else 1].unsqueeze(1).to_broadcast([P, 2, 256])
                return stt(out=PB[:, a % NPB], in0=side[:, 0:2, 0:256],
                           scalar=HEAD ** -0.5, in1=mask, op0=ALU.mult, op1=ALU.min).then_inc(scores_read, 1)

            def maxima(g):
                v.wait_ge(scores_read, 4 * g + 4)
                mx, a = MX[:, g % 2], 4 * g % NPB
                sinks = COLS[:, SINK + 8 * (g % 2):SINK + 8 * (g % 2) + 8]
                link(nc.vector.reduce_max(mx, PB[:, a:a + 4].rearrange("p a b k -> p (a b) k"), AX))
                link(tt(mx, mx, sinks, ALU.max))
                tt(SMK[:, g % 2], sinks, mx, ALU.subtract)
                link_to(ts(NMX[:, g % 2], mx, -1.0, None, ALU.mult), nmax_ready, g + 1)

            def attention(slot):
                for k in range(4):
                    for g in group_of(slot, N_SLOT0):
                        mask_scores(4 * g + k)
                    if k == 2:
                        for g in group_of(slot, N_SLOT0 + 1):
                            normalise(g)
                for g in group_of(slot, N_SLOT0):
                    maxima(g)

            def b_bar_lo():
                v.wait_ge(bh_ready, 1)
                link_to(tt(BHL[1][:], BB[:], BHL[0][:].bitcast(F32), ALU.subtract), bl_ready, 1)

            params_at = {8: (time_step, 0), 9: (time_step, 1), 10: (angles,), 12: (decay, 0), 13: (decay, 1),
                         14: (coefficients, 0), 16: (coefficients, 1), 17: (b_bar,), 18: (powers,),
                         20: (b_bar_lo,), 22: (rotation_start,)}
            for n in range(6, U_GATE):
                unit(n, 0)
                if n == 6:
                    v.wait_ge(std_ready, 1)
                    link(nc.vector.reciprocal(RSTD[:], RSTD[:]))
                    normed(Q[:, 0:2], 0)
                if n % 4 == 1 and 9 <= n <= 17:
                    b = (n - 5) // 4
                    normed(Q[:, 2 * b:2 * b + 2], b)
                if n % 4 == 3 and 7 <= n <= 19:
                    rope_q((n - 7) // 4)
                if n == 21:
                    normed(KV[:], 4)
                if n == 23:
                    rope_k()
                if n == N_SLOT0 + 2:
                    v.wait_ge(b_stored, 16 * 12)
                if n >= N_SLOT0 + 2:
                    attention(n - 2)
                if n in params_at:
                    params_at[n][0](*params_at[n][1:])
                if n in (25, 29, 33):
                    b = (n - 5) // 4
                    normed(U[:, 2 * b - 10:2 * b - 8], b)

            def mark(ins):
                ins.then_inc(dve_step, 1)
                step.n += 1
                return step.value()

            def scan_tile(c, q):
                s = c * 4 + q
                cos_, nsin = ROT_T[:, q % 2, 0], ROT_T[:, q % 2, 1]
                v.wait_ge(rot_ready, s + 1)
                v.wait_ge(bu_done, s + 1)
                tt(M1[:, 0], side[:, 0], cos_, ALU.mult)
                tt(M2[:, 0], side[:, 0], nsin, ALU.mult)
                w1 = mark(tt(M1[:, 1], side[:, 1], cos_, ALU.mult))
                tt(M2[:, 1], side[:, 1], nsin, ALU.mult).then_inc(bu_read, 1)
                v.wait_ge(dve_step, w1)
                w1 = mark(tt(WI[:, 1], M1[:, 1], M2[:, 0], ALU.add))
                v.wait_ge(bu_read, s + 1)
                w0 = mark(tt(WI[:, 0], M1[:, 0], M2[:, 1], ALU.subtract))
                r = MAG[:, bass.ds(s, 1)].to_broadcast([P, T])
                v.wait_ge(dve_step, w1)
                w1 = mark(nc.vector.tensor_tensor_scan(M1[:, 1], r, WI[:, 1], 0.0, ALU.mult, ALU.add))
                v.wait_ge(dve_step, w0)
                w0 = mark(nc.vector.tensor_tensor_scan(M1[:, 0], r, WI[:, 0], 0.0, ALU.mult, ALU.add))
                return lambda: rotate_back(s, q, cos_, nsin, w1, w0)

            def rotate_back(s, q, cos_, nsin, w1, w0):
                v.wait_ge(dve_step, w1)
                tt(WI[:, 1], M1[:, 1], cos_, ALU.mult)
                tt(M2[:, 1], M1[:, 1], nsin, ALU.mult)
                v.wait_ge(dve_step, w0)
                w1 = mark(tt(M2[:, 0], M1[:, 0], nsin, ALU.mult))
                w0 = mark(tt(WI[:, 0], M1[:, 0], cos_, ALU.mult))
                if not isinstance(s, int) or s >= 2:
                    v.wait_ge(c_done, s - 1)
                v.wait_ge(dve_step, w1)
                tt(SB[:, q % 2, 1], M2[:, 0], WI[:, 1], ALU.subtract)
                v.wait_ge(dve_step, w0)
                link_to(tt(SB[:, q % 2, 0], WI[:, 0], M2[:, 1], ALU.add), state_ready, s + 1)

            def gate(buf, b, end):
                v.wait_ge(unit_done, end)
                link_to(tt(GS[:, buf], main[:, 2 - 2 * buf:4 - 2 * buf], both(RSTD[:]), ALU.mult), bank_read, b + 1)

            def y_out(c, count):
                v.wait_ge(c_done, count * 4)
                link_to(stt(out=U[:, c], in0=U[:, c], scalar=COLS[:, bass.ds(c + D_SKIP, 1)], in1=side[:, 2],
                            op0=ALU.mult, op1=ALU.add), y_read, count)

            def u_lo(c):
                v.wait_ge(uh_ready, c + 1)
                tt(UHL[:, 1], U[:, c], UHL[:, 0].bitcast(F32), ALU.subtract).then_inc(ul_ready, 1)

            for j in range(8):
                unit(U_GATE, j)
                if j == 0:
                    u_lo(0)
                    attention(U_GATE - 2)
                if j == 1:
                    normed(U[:, 6:8], 8)
                if j >= 2 and j % 2 == 0:
                    if j == 2:
                        v.wait_ge(o_ready, 8)
                    back = scan_tile(0, j // 2 - 1)
                if j >= 3 and j % 2 == 1:
                    back()
                if j == 5:
                    gate(0, B_GATE, U_GATE + 4)
            per = 4 * 7
            with v.Fori(1, CT) as c:
                step.enter(c, 1, per)
                for j in range(8):
                    unit(U_GATE, j, c, 8)
                    if j == 0:
                        u_lo(c)
                        back = scan_tile(c - 1, 3)
                    if j == 1:
                        v.wait_ge(gate_stored[0], c * 16)
                        gate(1, c * 2 + (B_GATE - 1), c * 8 + U_GATE)
                    if j == 4:
                        y_out(c - 1, c)
                    if j >= 2 and j % 2 == 0:
                        back = scan_tile(c, j // 2 - 1)
                    if j % 2 == 1:
                        back()
                    if j == 5:
                        v.wait_ge(gate_stored[0], c * 16)
                        gate(0, c * 2 + B_GATE, c * 8 + (U_GATE + 4))
                step.leave(1, CT)
            scan_tile(CT - 1, 3)()
            unit(U_GLU, 0)
            v.wait_ge(gate_stored[1], 16 * (CT - 1))
            gate(1, B_GLU - 1, U_GLU)
            unit(U_GLU, 1)

            def y_lo(c):
                v.wait_ge(yh_ready, c + 1)
                tt(YL[:, c], U[:, c], YH[:, c].bitcast(F32), ALU.subtract).then_inc(yl_ready, 1)

            y_out(CT - 1, CT)
            for c in range(CT):
                y_lo(c)

            def glu(b):
                v.wait_ge(sig_ready, b + 1)
                if b >= 1:
                    v.wait_ge(osh_ready, b)
                link_to(tt(OT[:], main[:, 2 * ((B_GLU + b) % 2)], SG[:], ALU.mult), bank_read, B_GLU + b + 1)

            def glu_lo(b):
                v.wait_ge(osh_ready, b + 1)
                link_to(tt(OSL[:, b], OT[:], OSH[:, b].bitcast(F32), ALU.subtract), osl_ready, b + 1)

            for j in range(2, 16):
                unit(U_GLU, j)
                if j == 3:
                    glu(0)
                if j % 2 == 0 and j >= 4:
                    glu_lo((j - 4) // 2)
                if j % 2 == 1 and j >= 5:
                    glu((j - 3) // 2)
                if j in (4, 6):
                    for k in range(2 * j - 8, 2 * j - 4):
                        v.wait_ge(oah_ready, k + 1)
                        tt(OAL[:, k], Q[:, k], OAH[:, k].bitcast(F32), ALU.subtract).then_inc(oal_ready, 1)

            def branch_attn(p, b, end):
                v.wait_ge(unit_done, end)
                v.wait_ge(ga_landed, p * 16 + 16)
                link_to(tt(TA[:], main[:, 2:4], GA[:], ALU.mult), bank_read, b + 1)

            def branch_ssm(p, b, end):
                v.wait_ge(unit_done, end)
                v.wait_ge(gb_landed, p * 16 + 16)
                link_to(tt(TB[:], main[:, 0:2], GB[:], ALU.mult), bank_read, b + 1)
                link_to(tt(TB[:], TB[:], TA[:], ALU.add), br_ready, p + 1)

            def branch_lo(p):
                v.wait_ge(mh_ready, p + 1)
                t = bass.ds(p * 2, 2)
                link_to(tt(ML[:, t], TB[:], MH[:, t].bitcast(F32), ALU.subtract), ml_ready, p + 1)

            for j in range(4):
                unit(U_BR, j)
                if j == 0:
                    glu_lo(6)
                if j == 1:
                    glu(7)
                if j == 2:
                    glu_lo(7)
                if j == 3:
                    branch_attn(0, B_BR, U_BR + 2)
            with v.Fori(1, 8) as p:
                for j in range(4):
                    unit(U_BR, j, p, 4)
                    if j == 1:
                        branch_ssm(p - 1, p * 2 + (B_BR - 1), p * 4 + U_BR)
                    if j == 2:
                        branch_lo(p - 1)
                    if j == 3:
                        branch_attn(p, p * 2 + B_BR, p * 4 + (U_BR + 2))

            def mixed(i, b, end, buf):
                v.wait_ge(unit_done, end)
                link_to(nc.vector.tensor_copy(Z[:, bass.ds(i * 2, 2)], main[:, buf:buf + 2]), bank_read, b + 1)

            def add_squares(count):
                v.wait_ge(sq_ready, count)
                link_to(tt(SQS[:], SQS[:], SQ[:, 0], ALU.add), sq_used, count + 1)

            for j in range(8):
                unit(U_OUT, j)
                if j == 1:
                    branch_ssm(7, B_OUT - 1, U_OUT)
                if j == 2:
                    branch_lo(7)
                if j == 3:
                    link_to(nc.vector.memset(SQS[:], 0.0), sq_used, 1)
                if j == 5:
                    mixed(0, B_OUT, U_OUT + 4, 2)
                if j == 6:
                    add_squares(1)
            with v.Fori(1, 4) as i:
                for j in range(8):
                    unit(U_OUT, j, i, 8)
                    if j == 1:
                        mixed(i * 2 - 1, i * 2 + (B_OUT - 1), i * 8 + U_OUT, 0)
                    if j == 2:
                        add_squares(i * 2)
                    if j == 5:
                        mixed(i * 2, i * 2 + B_OUT, i * 8 + (U_OUT + 4), 2)
                    if j == 6:
                        add_squares(i * 2 + 1)
            link_to(tt(SQS[:, 0], SQS[:, 0], SQS[:, 1], ALU.add), sum_ready, 1)
            unit(U_UP, 0)
            unit(U_UP, 1)
            v.wait_ge(unit_done, U_UP)
            nc.vector.tensor_copy(Z[:, KT - 2], main[:, 0]).then_inc(last_tile, 1)
            nc.vector.tensor_copy(Z[:, KT - 1], main[:, 1]).then_inc(bank_read, 1)
            v.wait_ge(std_ready, 2)
            link(nc.vector.reciprocal(RSTD[:], RSTD[:]))

            for k in range(KT // 2):
                for t in (2 * k, 2 * k + 1):
                    ins = stt(out=Z[:, t], in0=Z[:, t], scalar=GAIN[:, 1, t:t + 1], in1=RSTD[:],
                              op0=ALU.mult, op1=ALU.mult)
                if k == 0:
                    v.wait_ge(xr_landed, 16 * KT // 4)
                link(ins)
                x1 = X1[:, 2 * k:2 * k + 2]
                tt(x1, x1, Z[:, 2 * k:2 * k + 2], ALU.add).then_inc(x1_ready, 1)
                if k % 2 == 1 and k // 2 < 2:
                    unit(U_UP, 2 + k // 2)

            def up(b, end, buf, count):
                v.wait_ge(unit_done, end)
                link_to(tt(TT[:], main[:, buf:buf + 2], both(RSTD[:]), ALU.mult), bank_read, b + 1)
                link_to(stt(out=AA[:], in0=TT[:], scalar=0.0, in1=TT[:], op0=ALU.max, op1=ALU.mult), a_ready, count)

            def up_lo(buf, half, count):
                v.wait_ge(ah_ready, count)
                link_to(tt(AL[:, buf, 2 * half:2 * half + 2], AA[:], AH[:, buf, 2 * half:2 * half + 2].bitcast(F32),
                           ALU.subtract), al_ready, count)

            def down(m, b, end, first=False):
                v.wait_ge(unit_done, end)
                o, ps = ACC[:, 2 * m:2 * m + 2], main[:, 2 - 2 * (m % 2):4 - 2 * (m % 2)]
                if first:
                    link_to(nc.vector.tensor_copy(o, ps), bank_read, b + 1)
                else:
                    link_to(tt(o, ps, o, ALU.add), bank_read, b + 1)

            def add_h2_squares(k):
                v.wait_ge(h2sq_ready, k + 1)
                link_to(tt(SQS[:], SQS[:], SQ[:, k % 2], ALU.add), h2sq_used, k + 2)

            for j in range(4, 8):
                unit(U_UP, j)
                if j == 4:
                    v.wait_ge(stat_done, 2)
                    link_to(nc.vector.memset(SQS[:], 0.0), h2sq_used, 1)
                if j in (4, 5):
                    for k in range(4 * j - 16, 4 * j - 12):
                        add_h2_squares(k)
                if j == 5:
                    tt(SQS[:, 0], SQS[:, 0], SQS[:, 1], ALU.add).then_inc(sum_ready, 1)
            v.wait_ge(std_ready, 3)
            link(nc.vector.reciprocal(RSTD[:], RSTD[:]))
            up(B_UP, U_UP + 4, 2, 1)
            up_lo(0, 0, 1)

            def group(j, buf, n0, b0, counts, first):
                if not first and j < 2:
                    down(6 + j, b0 - 2 + j, n0 - 1 + j)
                if j == 5 or j == 9:
                    h = j // 4 - 1
                    up(b0 + h, n0 + 4 + 4 * h, 2 - 2 * h, counts + h + 1)
                if j == 6 or j == 10:
                    h = j // 4 - 1
                    up_lo(buf, h, counts + h + 1)
                if j >= 10:
                    down(j - 10, b0 + (j - 8), n0 + (j - 1), first)

            for j in range(16):
                unit(U_MLP, j)
                if j == 1:
                    up(B_UP + 1, U_UP + 8, 0, 2)
                if j == 2:
                    up_lo(0, 1, 2)
                if j == 3:
                    link(nc.vector.memset(ACC[:, 12:16], 0.0))
                group(j, 1, U_MLP, B_MLP, 2, True)
            with v.Fori(0, (N_GROUP - 2) // 2) as i:
                for j in range(32):
                    unit(U_MLP + 16, j, i, 32)
                    h = j // 16
                    group(j % 16, h, i * 32 + (U_MLP + 16 + 16 * h), i * 20 + (B_MLP + 10 + 10 * h),
                          i * 4 + (4 + 2 * h), False)

            def add_final(m):
                v.wait_ge(fsq_ready, m + 1)
                link_to(tt(SQS[:], SQS[:], SQ[:, 0], ALU.add), fsq_used, m + 2)

            for j in range(8):
                unit(U_TAIL, j)
                if j < 2:
                    down(6 + j, B_TAIL - 2 + j, U_TAIL - 1 + j)
                else:
                    down(j - 2, B_TAIL + j - 2, U_TAIL + j - 1)
                if j == 2:
                    link_to(nc.vector.memset(SQS[:], 0.0), fsq_used, 1)
                if j >= 4:
                    add_final(j - 4)
            add_final(4)
            down(6, B_TAIL + 6, U_TAIL + 7)
            add_final(5)
            add_final(6)
            tt(SQS[:, 0], SQS[:, 0], SQS[:, 1], ALU.add).then_inc(sum_ready, 1)
            v.wait_ge(unit_done, N_UNIT)
            for t in range(2):
                o = ACC[:, KT - 2 + t]
                tt(o, main[:, t], o, ALU.add).then_inc(bank_read if t else last_tile, 1)
            v.wait_ge(bank_read, B_TAIL + 8)
            v.wait_ge(std_ready, 4)
            link(nc.vector.reciprocal(RSTD[:], RSTD[:]))
            v.wait_ge(x1_back, 16 * KT // 4)
            for k in range(KT // 2):
                for t in (2 * k, 2 * k + 1):
                    ins = stt(out=ACC[:, t], in0=ACC[:, t], scalar=GAIN[:, 3, t:t + 1], in1=RSTD[:],
                              op0=ALU.mult, op1=ALU.mult)
                ins.then_inc(product_ready, 1)
                if ADDER[k] == "DVE":
                    v.wait_ge(product_ready, k + 1)
                    o = ACC[:, 2 * k:2 * k + 2]
                    tt(o, o, X1F[:, 2 * k:2 * k + 2], ALU.add).then_inc(out_ready["DVE"], 1)

        @block.tensor
        def _(pe):
            mm = nc.tensor.matmul

            def product(n, s, b_odd, xh, xl, k0, first, last, between=None, ready=None):
                pe.wait_ge(lo_ready, n + 1)
                for k in range(4):
                    if ready is not None:
                        ready(k)
                    for m in range(2):
                        wh, wl = WH[:, s, k, m * P:m * P + P], WL[:, s, k, m * P:m * P + P]
                        o = main[:, 2 * b_odd + m]
                        mm(o, wh, xh[:, k0 + k], start=first and k == 0, stop=False)
                        mm(o, wh, xl[:, k0 + k], start=False, stop=False)
                        ins = mm(o, wl, xh[:, k0 + k], start=False, stop=last and k == 3)
                    if k == 3:
                        ins.then_inc(unit_done, 1)
                    if between is not None:
                        between(k)

            def take_bank(b):
                if not isinstance(b, int) or b >= 2:
                    pe.wait_ge(bank_read, b - 1)

            for n in range(4):
                product(n, n, 0, HH, HL, 4 * n, n == 0, n == 3, ready=lambda k: pe.wait_ge(xl_ready, 4 * n + k + 1))

            def rope(x, b, tiles):
                pe.wait_ge(bank_read, b + 1)
                pe.wait_ge(rope_free, b + 1)
                for t in range(tiles):
                    ins = mm(side[:, t], PERM[:], x(t), start=True, stop=True)
                ins.then_inc(rope_mm, 1)

            for i in range(2):
                for j in range(8):
                    if j % 4 == 0:
                        take_bank(i * 2 + (1 + j // 4))
                    product(i * 8 + (4 + j), j % 4, 1 - j // 4, HH, HL, 4 * (j % 4), j % 4 == 0, j % 4 == 3)
                    if i == 0 and j == 0:
                        pe.wait_ge(ones_set, 1)
                        pe.wait_ge(xsum_step, 5)
                        mm(side[:, 3], ONES[:], SUM0[:, 0], start=True, stop=True).then_inc(stat_done, 1)
                    if j in (1, 5):
                        h = j // 4
                        if i == 0 and j == 1:
                            pe.wait_ge(consts_landed, 64)
                        rope(lambda t: Q[:, i * 4 + (2 * h + t)], i * 2 + h, 2)

            def attention(slot, k):
                for g in group_of(slot, N_SLOT0 + 3):
                    a, n = 4 * g + k, g // 2
                    pe.wait_ge(pt_ready, a + 1)
                    if g >= 1:
                        pe.wait_ge(o_ready, g)
                    for b in range(2):
                        for kb in range(2):
                            ins = mm(side[HEAD * b:HEAD * b + HEAD, 3, k * P:k * P + P],
                                     VTOK[:, n + kb, HEAD * b:HEAD * b + HEAD],
                                     PTB[:, a % 4, (2 * b + kb) * P:(2 * b + kb + 1) * P],
                                     start=kb == 0, stop=kb == 1)
                    ins.then_inc(pv_done, 1)
                for g in group_of(slot, N_SLOT0):
                    a, n = 4 * g + k, g // 2
                    if a >= 1:
                        pe.wait_ge(scores_read, a)
                    for b in range(2):
                        r = slice(HEAD * b, HEAD * b + HEAD)
                        ins = mm(side[:, b, 0:256], Q[r, a % 8, n * P:n * P + P],
                                 KTOK[r, n * P:n * P + 2 * P], start=True, stop=True)
                    ins.then_inc(scores_done, 1)
                for g in group_of(slot, N_SLOT0 + 2):
                    a = 4 * g + k
                    pe.wait_ge(probs_ready, g + 1)
                    if a >= 1:
                        pe.wait_ge(pt_ready, a)
                    for b in range(2):
                        for kb in range(2):
                            ins = nc.tensor.transpose(side[:, 2, (2 * b + kb) * P:(2 * b + kb + 1) * P],
                                                      PB[:, a % NPB, b, kb * P:kb * P + P], IDENT[:])
                    ins.then_inc(trans_done, 1)

            for n in range(U_U, U_GATE):
                b, j = 5 + (n - U_U) // 4, (n - U_U) % 4
                if j == 0:
                    take_bank(b)
                if n == N_SLOT0:
                    pe.wait_ge(rope_free, 6)
                    pe.wait_ge(v_ready, 1)
                product(n, n % 4, b % 2, HH, HL, 4 * j, j == 0, j == 3,
                        (lambda k: attention(n, k)) if n >= N_SLOT0 else None)
                if n == 21:
                    rope(lambda t: KV[:, 0], 4, 1)
                    for t in range(4):
                        ins = nc.tensor.transpose(side[:, 2, t * P:t * P + P], KV[:, 1, t * P:t * P + P], IDENT[:])
                    ins.then_inc(vt_done, 1)

            def bu(c, q):
                s = c * 4 + q
                pe.wait_ge(rows_ready, s + 1)
                if not isinstance(s, int) or s >= 1:
                    pe.wait_ge(bu_read, s)
                mm(side[:, 0], BW[0:96, 0], US[0:96], start=True, stop=True)
                mm(side[:, 1], BW[0:96, 1], US[0:96], start=True, stop=True).then_inc(bu_done, 1)

            def cs(c, q):
                s = c * 4 + q
                if q % 2 == 0:
                    pe.wait_ge(c_landed[q // 2], c * 16 + 16)
                if q == 0:
                    if not isinstance(c, int) or c >= 1:
                        pe.wait_ge(y_read, c)
                pe.wait_ge(state_ready, s + 1)
                r = slice(32 * q, 32 * q + 32)
                mm(side[r, 2], CST[:, q, 0], SB[:, q % 2, 0], start=True, stop=False)
                mm(side[r, 2], CST[:, q, 1], SB[:, q % 2, 1], start=False, stop=True).then_inc(c_done, 1)

            def gates(c, first):
                for j in range(8):
                    if j % 4 == 0:
                        take_bank(c * 2 + (B_GATE + j // 4))
                    product(c * 8 + (U_GATE + j), j % 4, 1 - j // 4, HH, HL, 4 * (j % 4), j % 4 == 0, j % 4 == 3)
                    if j % 2 == 0:
                        bu(c, j // 2)
                        if j >= 4:
                            cs(c, j // 2 - 2)
                        elif not first:
                            cs(c - 1, j // 2 + 2)

            gates(0, True)
            with pe.Fori(1, CT) as c:
                gates(c, False)
            cs(CT - 1, 2)
            cs(CT - 1, 3)

            def glu(i, first):
                for j in range(4):
                    if j % 2 == 0:
                        take_bank(i * 2 + (B_GLU + j // 2))
                    product(i * 4 + (U_GLU + j), j, 1 - j // 2, YH, YL, 4 * (j % 2), j % 2 == 0, j % 2 == 1,
                            ready=(lambda k: pe.wait_ge(yl_ready, 4 * j + k + 1)) if first and j < 2 else None)

            glu(0, True)
            with pe.Fori(1, 4) as i:
                glu(i, False)

            def branches(p, first):
                for j in range(4):
                    if j % 2 == 0:
                        take_bank(p * 2 + (B_BR + j // 2))
                    if first and j < 2:
                        pe.wait_ge(oal_ready, 4 * j + 4)
                    if first and j >= 2:
                        pe.wait_ge(osl_ready, 4 * (j - 1))
                    xh, xl = (OAH, OAL) if j < 2 else (OSH, OSL)
                    product(p * 4 + (U_BR + j), j, 1 - j // 2, xh, xl, 4 * (j % 2), j % 2 == 0, j % 2 == 1)

            branches(0, True)
            with pe.Fori(1, 8) as p:
                branches(p, False)

            def project(i, first):
                for j in range(8):
                    if j % 4 == 0:
                        take_bank(i * 2 + (B_OUT + j // 4))
                    if first and j < 4:
                        pe.wait_ge(ml_ready, 2 * j + 2)
                    product(i * 8 + (U_OUT + j), j % 4, 1 - j // 4, MH, ML, 4 * (j % 4), j % 4 == 0, j % 4 == 3)

            project(0, True)
            with pe.Fori(1, 4) as i:
                project(i, False)

            def last_norm(n, count):
                pe.wait_ge(sum_ready, count)
                mm(side[:, 3], ONES[:], SQS[:, 0], start=True, stop=False)
                for t in range(2):
                    pe.wait_ge(last_sq, 2 * n + t + 1)
                    ins = mm(side[:, 3], ONES[:], SQ[:, 1, t], start=False, stop=t == 1)
                ins.then_inc(stat_done, 1)

            last_norm(0, 1)

            def up(n0, b0, first):
                for j in range(8):
                    if j % 4 == 0:
                        take_bank(b0 + j // 4)
                    product(n0 + j, j % 4, 1 - j // 4, MH, ML, 4 * (j % 4), j % 4 == 0, j % 4 == 3,
                            ready=(lambda k: pe.wait_ge(h2l_ready, 2 * j + k // 2 + 1)) if first and j < 4 else None)
                    if first and j == 5:
                        pe.wait_ge(sum_ready, 2)
                        mm(side[:, 3], ONES[:], SQS[:, 0], start=True, stop=True).then_inc(stat_done, 1)

            def down(n0, b0, buf, halves):
                for m in range(8):
                    take_bank(b0 + m)
                    if m == 0:
                        pe.wait_ge(al_ready, halves)
                    product(n0 + m, m % 4, 1 - m % 2, AH[:, buf], AL[:, buf], 0, True, True)

            up(U_UP, B_UP, True)
            up(U_MLP, B_MLP, False)
            down(U_MLP + 8, B_MLP + 2, 0, 2)
            with pe.Fori(0, (N_GROUP - 2) // 2) as i:
                for h in range(2):
                    n0, b0 = i * 32 + (U_MLP + 16 + 16 * h), i * 20 + (B_MLP + 10 + 10 * h)
                    up(n0, b0, False)
                    down(n0 + 8, b0 + 2, 1 - h, i * 4 + (4 + 2 * h))
            down(U_TAIL, B_TAIL, 1, 2 * N_GROUP)
            last_norm(1, 3)


def units(w, blocks, kts):
    t = w.reshape(w.shape[0] // P, P, w.shape[1] // P, P)
    got = [t[k:k + 4][:, :, list(b)].transpose(1, 0, 2, 3).reshape(P, 1024)
           for b in blocks for k in range(kts[0], kts[1], 4)]
    return got


def in_pairs(n):
    return [(2 * b, 2 * b + 1) for b in range(n)]


def head_order():
    return np.concatenate([np.arange(h * HEAD, h * HEAD + HEAD) for i in range(8) for h in (i, 8 + i)])


def stream(w_in, w_glu, w_branch, w_out, w_up, w_down):
    q = N_Q * HEAD
    kv = 2 * N_KV * HEAD
    order = head_order()
    g = []
    g += units(w_in[:, :q][:, order], in_pairs(4), (0, KT))
    g += units(w_in[:, q:q + kv], in_pairs(1), (0, KT))
    g += units(w_in[:, q + kv:q + kv + SSM_W], in_pairs(4), (0, KT))
    g += units(w_in[:, q + kv + SSM_W:], in_pairs(16), (0, KT))
    g += units(w_glu, [(b, 8 + b) for b in range(8)], (0, 8))
    attn, ssm = w_branch[:q][order], w_branch[q:]
    for p in range(8):
        g += units(attn, [(2 * p, 2 * p + 1)], (0, 8)) + units(ssm, [(2 * p, 2 * p + 1)], (0, 8))
    g += units(w_out, in_pairs(8), (0, KT))
    up = [units(w_up, [(4 * h, 4 * h + 1), (4 * h + 2, 4 * h + 3)], (0, KT)) for h in range(N_GROUP)]
    down = [units(w_down, in_pairs(8), (4 * h, 4 * h + 4)) for h in range(N_GROUP)]
    g += up[0]
    for h in range(1, N_GROUP):
        g += up[h] + down[h - 1]
    g += down[-1]
    assert len(g) == N_UNIT
    return np.stack(g)


def by_partition(v):
    return v.reshape(-1, P).T


def shape_constants():
    half = ROT // 2
    inv = np.float32(THETA) ** (-np.arange(half, dtype=np.float32) * np.float32(2.0) / np.float32(ROT))
    ang = np.arange(T, dtype=np.float32)[None, :] * inv[:, None].astype(np.float32)
    cos, sin = np.ones((P, T), np.float32), np.zeros((P, T), np.float32)
    perm = np.zeros((P, P), np.float32)
    for h in (0, HEAD):
        for d in range(half):
            for e in (d, d + half):
                cos[h + e], sin[h + e] = np.cos(ang[d]), np.sin(ang[d])
            perm[h + d + half, h + d] = -1.0
            perm[h + d, h + d + half] = 1.0
    far = np.finfo(np.float32).max
    query, key = np.arange(P)[:, None], np.arange(2 * P)[None, :]
    rel = query + P - key
    inside = (rel >= 0) & (rel < P)
    first = np.where(inside & (key >= P), far, -far).astype(np.float32)
    rest = np.where(inside, far, -far).astype(np.float32)
    return np.concatenate([cos, sin, perm, np.eye(P, dtype=np.float32), first, rest], axis=1)


def parameter_rows(x):
    by_channel = np.repeat(x.reshape(CT, 8, SSM_S).transpose(1, 0, 2)[:, None], SSM_C, axis=1).reshape(P, NW)
    by_state = x.reshape(ST, P).T
    return np.concatenate([by_channel, by_state], axis=1)


def padded_b(b):
    out = np.zeros((4, 2, SSM_C, CT, 2, SSM_S), np.float32)
    x = b.reshape(CT, 4, 2, SSM_S, SSM_C)
    for g in range(2):
        out[:, g, :, :, g] = x[:, :, g].transpose(1, 3, 0, 2)
    return out.reshape(P, CT * P)


def padded_c(re, im):
    out = np.zeros((CT, 2, SSM_S, 4, 2, 2, SSM_C), np.float32)
    for r, c in enumerate((re, im)):
        x = c.reshape(CT, 4, 2, SSM_C, SSM_S)
        for g in range(2):
            out[:, g, :, :, r, g] = x[:, :, g].transpose(0, 3, 1, 2)
    return out.reshape(CT, P, 256)


def kernel(**inputs):
    import concourse.bacc as bacc
    from concourse.bass_utils import run_bass_kernel_spmd

    a = {k: np.asarray(v) for k, v in inputs.items()}
    one = {k: v[0] for k, v in a.items() if k != "x"}
    heads = [h for i in range(8) for h in (i, 8 + i)]
    cols = np.zeros((P, 32), np.float32)
    cols[:, 0:8] = by_partition(one["d_skip"].reshape(-1))
    cols[:, 8:24] = one["sinks"][heads][None, :]
    cols[:, 24] = EPS
    arrays = {
        "wstream": stream(one["w_in"], one["w_glu"], one["w_branch"], one["w_out"], one["w_up"], one["w_down"]),
        "x_t": np.ascontiguousarray(a["x"][0].T).reshape(KT, P, T),
        "gains": np.concatenate([by_partition(one[k]) for k in
                                 ("norm_mix_pre", "norm_mix_post", "norm_mlp_pre", "norm_mlp_post")], axis=1),
        "params": np.stack([parameter_rows(one["lam_re"]), parameter_rows(one["lam_im"]),
                            parameter_rows(np.repeat(one["log_dt"][:, None], SSM_S, axis=1))]),
        "b_pad": np.stack([padded_b(one["b_re"]), padded_b(one["b_im"])]),
        "c_pad": padded_c(one["c_re"], one["c_im"]),
        "consts": shape_constants(),
        "cols": cols,
    }
    arrays = {k: np.ascontiguousarray(v) for k, v in arrays.items()}
    nc = bacc.Bacc("TRN2", target_bir_lowering=False, num_devices=1)
    args = [nc.dram_tensor(k, v.shape, mybir.dt.from_np(v.dtype), kind="ExternalInput").ap()
            for k, v in arrays.items()]
    out = nc.dram_tensor("out_t", (KT // 2, P, 2 * T), F32, kind="ExternalOutput").ap()
    build(nc, *args, out)
    got = run_bass_kernel_spmd(nc, [arrays], core_ids=[0]).results[0]["out_t"]
    y = got.reshape(KT // 2, P, 2, T).transpose(0, 2, 1, 3).reshape(D, T)
    return np.ascontiguousarray(y.T)[None]
```
